# Optimizing a Trainium2 kernel written in Bass

```python
import math
import jax
import jax.numpy as jnp
from jax import lax
import numpy as np

D_MODEL = 2048
BATCH = 1
SEQ = 512
DEPTH = 1

GRID_W = 64
CTX_LEN = 256
N_MIXERS = 4
NORM_EPS = 1e-6
D_FF = 4 * D_MODEL
N_ADA = 6
FNO_GROUPS = 4
GMLP_CHUNK = 128
GMLP_HEADS = 16
GMLP_WIDTH = D_MODEL
DIFF_HEADS = 8
DIFF_HEAD_DIM = D_MODEL // DIFF_HEADS // 2
DIFF_BLOCK_Q = 128
ROPE_THETA = 10000.0
GLA_HEADS = 4
GLA_DK = D_MODEL // 2
GLA_DV = D_MODEL
GLA_DK_HEAD = GLA_DK // GLA_HEADS
GLA_DV_HEAD = GLA_DV // GLA_HEADS
GLA_GATE_RANK = 16
GLA_TAU = 16.0
GLA_CHUNK = 64
GLA_IN = 2 * GLA_DK + 2 * GLA_DV + 2 * GLA_GATE_RANK

kernel_name = 'hybrid_interleaved_fourier_gmlp_diffattn_gla_dit'

def _layer_count(kind):
    return len(range(kind, DEPTH, N_MIXERS))

def _rmsnorm(x, g, eps=NORM_EPS):
    xf = x.astype(jnp.float32)
    y = xf * lax.rsqrt(jnp.mean(xf * xf, axis=-1, keepdims=True) + eps)
    return (y * g.astype(jnp.float32)).astype(x.dtype)

def _layernorm(x, g, b, eps=1e-5):
    xf = x.astype(jnp.float32)
    mu = jnp.mean(xf, axis=-1, keepdims=True)
    xc = xf - mu
    var = jnp.mean(xc * xc, axis=-1, keepdims=True)
    return (xc * lax.rsqrt(var + eps) * g.astype(jnp.float32) + b.astype(jnp.float32)).astype(x.dtype)

def _modulate(x, g, shift, scale):
    return _rmsnorm(x, g) * (1 + scale) + shift

def _sq_relu_mlp(h, w_in, w_out):
    return jnp.square(jax.nn.relu(h @ w_in)) @ w_out

def fourier_mix(h, w_out):
    b, n, d = h.shape
    hg = h.astype(jnp.float32).reshape(b, n, FNO_GROUPS, d // FNO_GROUPS)
    f = jnp.fft.fftn(hg, axes=(1, 3), norm='ortho').real
    return f.reshape(b, n, d).astype(h.dtype) @ w_out

def chunk_gmlp(h, w_in, ln_g, ln_b, w_s, b_s, w_out):
    b, n, _ = h.shape
    z = jax.nn.gelu(h @ w_in, approximate=False)
    u, v = jnp.split(z, 2, axis=-1)
    v = _layernorm(v, ln_g, ln_b)
    vc = v.reshape(b, n // GMLP_CHUNK, GMLP_CHUNK, GMLP_HEADS, GMLP_WIDTH // GMLP_HEADS)
    s = jnp.einsum('hpq,bcqhe->bcphe', w_s, vc) + b_s.T[:, :, None]
    return (u * s.reshape(b, n, GMLP_WIDTH)) @ w_out

def _axial_rope(n, head_dim):
    rows = n // GRID_W
    row = jnp.broadcast_to(jnp.arange(rows)[:, None], (rows, GRID_W)).reshape(-1).astype(jnp.float32)
    col = jnp.broadcast_to(jnp.arange(GRID_W)[None, :], (rows, GRID_W)).reshape(-1).astype(jnp.float32)
    n_freq = head_dim // 4
    inv = ROPE_THETA ** (-jnp.arange(n_freq, dtype=jnp.float32) / n_freq)
    ang = jnp.concatenate([row[:, None] * inv, col[:, None] * inv], axis=-1)
    return jnp.cos(ang), jnp.sin(ang)

def _apply_rope(x, cos, sin):
    x1, x2 = jnp.split(x, 2, axis=-1)
    cos = cos.astype(x.dtype)
    sin = sin.astype(x.dtype)
    return jnp.concatenate([x1 * cos - x2 * sin, x1 * sin + x2 * cos], axis=-1)

def diff_attention(hx, hc, w_in, lam_vecs, subln_g, w_out, lam_init):
    b, n, d = hx.shape
    nh, hd = DIFF_HEADS, DIFF_HEAD_DIM

    def qkv(h):
        l = h.shape[1]
        q, k, v = jnp.split(h @ w_in, 3, axis=-1)
        q = q.reshape(b, l, nh, 2, hd).transpose(0, 2, 3, 1, 4)
        k = k.reshape(b, l, nh, 2, hd).transpose(0, 2, 3, 1, 4)
        v = v.reshape(b, l, nh, 2 * hd).transpose(0, 2, 1, 3)
        return q, k, v

    qx, kx, vx = qkv(hx)
    qc, kc, vc = qkv(hc)
    cos, sin = _axial_rope(n, hd)
    qx = _apply_rope(qx, cos, sin)
    kx = _apply_rope(kx, cos, sin)
    lam = (jnp.exp(jnp.sum(lam_vecs[0].astype(jnp.float32) * lam_vecs[1].astype(jnp.float32)))
           - jnp.exp(jnp.sum(lam_vecs[2].astype(jnp.float32) * lam_vecs[3].astype(jnp.float32)))
           + lam_init)
    scale = hd ** -0.5

    def attend(q, k, v):
        s = jnp.einsum('bhcqd,bhckd->bhcqk', q, k, preferred_element_type=jnp.float32) * scale
        p = jax.nn.softmax(s, axis=-1)
        a = p[:, :, 0] - lam * p[:, :, 1]
        return jnp.einsum('bhqk,bhkv->bhqv', a.astype(v.dtype), v)

    oc = attend(qc, kc, vc)
    k_all = jnp.concatenate([kx, kc], axis=3)
    v_all = jnp.concatenate([vx, vc], axis=2)
    nb = n // DIFF_BLOCK_Q
    q_blocks = jnp.moveaxis(qx.reshape(b, nh, 2, nb, DIFF_BLOCK_Q, hd), 3, 0)
    ox = lax.map(lambda qb: attend(qb, k_all, v_all), q_blocks)
    ox = jnp.moveaxis(ox, 0, 2).reshape(b, nh, n, 2 * hd)

    def finish(o):
        o = _rmsnorm(o, subln_g) * (1 - lam_init)
        return o.transpose(0, 2, 1, 3).reshape(b, o.shape[2], d) @ w_out

    return finish(ox), finish(oc)

def _gla_scan(q, k, v, g, s0):
    b, nh, l, _ = q.shape
    nc = l // GLA_CHUNK
    mask = jnp.tril(jnp.ones((GLA_CHUNK, GLA_CHUNK), dtype=bool))

    def to_chunks(t):
        return jnp.moveaxis(t.reshape(b, nh, nc, GLA_CHUNK, t.shape[-1]), 2, 0)

    def step(s, inp):
        qc, kc, vc, gc = inp
        bcum = jnp.cumsum(gc, axis=-2)
        blast = bcum[..., -1:, :]
        q_dec = qc * jnp.exp(bcum)
        k_inv = kc * jnp.exp(-bcum)
        k_tail = kc * jnp.exp(blast - bcum)
        att = jnp.where(mask, jnp.einsum('bhtd,bhsd->bhts', q_dec, k_inv), 0.0)
        o = jnp.einsum('bhtd,bhdv->bhtv', q_dec, s) + jnp.einsum('bhts,bhsv->bhtv', att, vc)
        s_new = jnp.exp(blast)[..., 0, :, None] * s + jnp.einsum('bhsd,bhsv->bhdv', k_tail, vc)
        return s_new, o

    s_final, o = lax.scan(step, s0, (to_chunks(q), to_chunks(k), to_chunks(v), to_chunks(g)))
    return jnp.moveaxis(o, 0, 2).reshape(b, nh, l, v.shape[-1]), s_final

def _gla_final_state(k, v, g):
    bcum = jnp.cumsum(g, axis=2)
    return jnp.einsum('bhsd,bhsv->bhdv', k * jnp.exp(bcum[:, :, -1:] - bcum), v)

def gla_mix(hx, hc, w_in, w_gate_up, b_gate, norm_g, w_out, need_ctx_out):
    b = hx.shape[0]
    splits = [GLA_DK, 2 * GLA_DK, 2 * GLA_DK + GLA_DV, 2 * GLA_DK + 2 * GLA_DV,
              2 * GLA_DK + 2 * GLA_DV + GLA_GATE_RANK]

    def project(h):
        l = h.shape[1]

        def heads(t, e):
            return t.reshape(b, l, GLA_HEADS, e).transpose(0, 2, 1, 3).astype(jnp.float32)

        q, k, v, r, gd_f, gd_b = jnp.split(h @ w_in, splits, axis=-1)

        def log_gate(gd, j):
            z = (gd @ w_gate_up[j] + b_gate[j]).astype(jnp.float32)
            return heads(jax.nn.log_sigmoid(z) / GLA_TAU, GLA_DK_HEAD)

        q = heads(q, GLA_DK_HEAD) * (GLA_DK_HEAD ** -0.5)
        return q, heads(k, GLA_DK_HEAD), heads(v, GLA_DV_HEAD), r, log_gate(gd_f, 0), log_gate(gd_b, 1)

    def flip(t):
        return jnp.flip(t, axis=2)

    def finish(o, r):
        o = _rmsnorm(o.astype(r.dtype), norm_g)
        l = o.shape[2]
        o = o.transpose(0, 2, 1, 3).reshape(b, l, GLA_DV)
        return (o * jax.nn.silu(r)) @ w_out

    qx, kx, vx, rx, gfx, gbx = project(hx)
    qc, kc, vc, rc, gfc, gbc = project(hc)
    zeros = jnp.zeros((b, GLA_HEADS, GLA_DK_HEAD, GLA_DV_HEAD), jnp.float32)
    if need_ctx_out:
        oc_f, sc_f = _gla_scan(qc, kc, vc, gfc, zeros)
        oc_b, sc_b = _gla_scan(flip(qc), flip(kc), flip(vc), flip(gbc), zeros)
        oc = finish(oc_f + flip(oc_b), rc)
    else:
        sc_f = _gla_final_state(kc, vc, gfc)
        sc_b = _gla_final_state(flip(kc), flip(vc), flip(gbc))
        oc = None
    ox_f, _ = _gla_scan(qx, kx, vx, gfx, sc_f)
    ox_b, _ = _gla_scan(flip(qx), flip(kx), flip(vx), flip(gbx), sc_b)
    return finish(ox_f + flip(ox_b), rx), oc

def setup_inputs(seed: int = 0) -> dict:
    key = jax.random.key(seed)
    keys = iter(jax.random.split(key, 32))
    f32 = jnp.float32
    d = D_MODEL

    def nrm(shape, scale):
        return jax.random.normal(next(keys), shape, f32) * scale

    def gain(shape):
        return 1.0 + 0.05 * jax.random.normal(next(keys), shape, f32)

    n_a, n_b, n_c, n_d = (_layer_count(m) for m in range(N_MIXERS))
    return {
        'x': nrm((BATCH, SEQ, d), 1.0),
        'c': nrm((BATCH, d), 1.0),
        'ctx': nrm((BATCH, CTX_LEN, d), 1.0),
        'c_ctx': nrm((d,), 1.0),
        'w_ada': nrm((DEPTH, d, N_ADA * d), 0.5 * d ** -0.5),
        'b_ada': nrm((DEPTH, N_ADA * d), 0.02),
        'g_norm_mix': gain((DEPTH, d)),
        'g_norm_ffn': gain((DEPTH, d)),
        'w_ffn_in': nrm((DEPTH, d, D_FF), d ** -0.5),
        'w_ffn_out': nrm((DEPTH, D_FF, d), D_FF ** -0.5),
        'g_final': gain((d,)),
        'fno_w_out': nrm((n_a, d, d), d ** -0.5),
        'gmlp_w_in': nrm((n_b, d, 2 * GMLP_WIDTH), d ** -0.5),
        'gmlp_ln_g': gain((n_b, GMLP_WIDTH)),
        'gmlp_ln_b': nrm((n_b, GMLP_WIDTH), 0.02),
        'gmlp_w_s': nrm((n_b, GMLP_HEADS, GMLP_CHUNK, GMLP_CHUNK), GMLP_CHUNK ** -0.5),
        'gmlp_b_s': gain((n_b, GMLP_HEADS, GMLP_CHUNK)),
        'gmlp_w_out': nrm((n_b, GMLP_WIDTH, d), GMLP_WIDTH ** -0.5),
        'diff_w_in': nrm((n_c, d, 3 * d), d ** -0.5),
        'diff_lambda': nrm((n_c, 4, DIFF_HEAD_DIM), 0.1),
        'diff_subln_g': gain((n_c, 2 * DIFF_HEAD_DIM)),
        'diff_w_out': nrm((n_c, d, d), d ** -0.5),
        'gla_w_in': nrm((n_d, d, GLA_IN), d ** -0.5),
        'gla_w_gate_up': nrm((n_d, 2, GLA_GATE_RANK, GLA_DK), GLA_GATE_RANK ** -0.5),
        'gla_b_gate': nrm((n_d, 2, GLA_DK), 0.1),
        'gla_norm_g': gain((n_d, GLA_DV_HEAD)),
        'gla_w_out': nrm((n_d, GLA_DV, d), GLA_DV ** -0.5),
    }

def reference(x, c, ctx, c_ctx, w_ada, b_ada, g_norm_mix, g_norm_ffn, w_ffn_in, w_ffn_out, g_final,
              fno_w_out, gmlp_w_in, gmlp_ln_g, gmlp_ln_b, gmlp_w_s, gmlp_b_s, gmlp_w_out,
              diff_w_in, diff_lambda, diff_subln_g, diff_w_out,
              gla_w_in, gla_w_gate_up, gla_b_gate, gla_norm_g, gla_w_out):
    silu_c = jax.nn.silu(c)
    silu_cc = jax.nn.silu(c_ctx)
    for i in range(DEPTH):
        kind, j = i % N_MIXERS, i // N_MIXERS
        last = i == DEPTH - 1
        mod_x = (silu_c @ w_ada[i] + b_ada[i])[:, None, :]
        mod_c = silu_cc @ w_ada[i] + b_ada[i]
        sh1, sc1, ga1, sh2, sc2, ga2 = jnp.split(mod_x, N_ADA, axis=-1)
        ch1, cs1, cg1, ch2, cs2, cg2 = jnp.split(mod_c, N_ADA, axis=-1)
        hx = _modulate(x, g_norm_mix[i], sh1, sc1)
        hc = _modulate(ctx, g_norm_mix[i], ch1, cs1)
        if kind == 0:
            ox, oc = fourier_mix(hx, fno_w_out[j]), fourier_mix(hc, fno_w_out[j])
        elif kind == 1:
            gp = (gmlp_w_in[j], gmlp_ln_g[j], gmlp_ln_b[j], gmlp_w_s[j], gmlp_b_s[j], gmlp_w_out[j])
            ox, oc = chunk_gmlp(hx, *gp), chunk_gmlp(hc, *gp)
        elif kind == 2:
            lam_init = 0.8 - 0.6 * math.exp(-0.3 * i)
            ox, oc = diff_attention(hx, hc, diff_w_in[j], diff_lambda[j], diff_subln_g[j],
                                    diff_w_out[j], lam_init)
        else:
            ox, oc = gla_mix(hx, hc, gla_w_in[j], gla_w_gate_up[j], gla_b_gate[j], gla_norm_g[j],
                             gla_w_out[j], not last)
        x = x + ga1 * ox
        x = x + ga2 * _sq_relu_mlp(_modulate(x, g_norm_ffn[i], sh2, sc2), w_ffn_in[i], w_ffn_out[i])
        if not last:
            ctx = ctx + cg1 * oc
            ctx = ctx + cg2 * _sq_relu_mlp(_modulate(ctx, g_norm_ffn[i], ch2, cs2), w_ffn_in[i], w_ffn_out[i])
    return _rmsnorm(x, g_final)


_drawn_inputs = setup_inputs


def setup_inputs(seed=0):
    import zlib

    import numpy as np

    out = dict(_drawn_inputs(seed))
    spreads = {}
    factors = {'g_norm_mix': 4.867, 'g_norm_ffn': 3.326}
    for name, (base, spread) in spreads.items():
        noise = np.random.default_rng([zlib.crc32(name.encode()), seed]).standard_normal(out[name].shape)
        drawn = base * np.exp(spread * noise) if base else spread * noise
        out[name] = jnp.asarray(drawn.astype(out[name].dtype))
    for name, factor in factors.items():
        out[name] = (out[name] * factor).astype(out[name].dtype)
    return out
```

```python
import math
from contextlib import ExitStack

import numpy as np

import concourse.bass as bass
from concourse import mybir


def fourier_ffn_block(nc, x, c, w_ada, vectors, bias_rows, g_final, w_mix, w_ffn_in, w_ffn_out,
                      seq_table, chan_table, identity, out):
    F32, F32R = mybir.dt.float32, mybir.dt.float32r
    ALU, ACT = mybir.AluOpType, mybir.ActivationFunctionType

    P = 128
    N, D = x.shape
    FF = w_ffn_in.shape[1]
    TT = N // P
    DT = D // P
    GROUPS = 4
    GD = D // GROUPS
    GT = GD // P
    HALF = N // 2
    COLS = 512
    UK = 4
    UNIT = UK * COLS
    DB = D // COLS
    CH = 1024
    CHUNKS = FF // CH
    HT = CH // P
    RAW = 4
    WS = 2
    EPS = 1e-6
    NORM = 1.0 / math.sqrt(N * GD)
    assert N == GD == COLS and D == UNIT

    SHIFT1, SCALE1, GATE1, SHIFT2, SCALE2, GATE2 = range(6)
    units = [("seq", i) for i in range(2)]
    units += [("ada", SCALE1, k) for k in range(DT)]
    units += [("chan", i) for i in range(4)]
    units += [("ada", SHIFT1, k) for k in range(DT)]
    units += [("ada", GATE1, k) for k in range(DT)]
    second = [("ada", SHIFT2, k) for k in range(DT)] + [("ada", SCALE2, k) for k in range(DT)]
    mix_units = [(d, q) for d in range(DB) for q in range(DT // UK)]
    per_mix = len(second) // len(mix_units)
    for i, (d, q) in enumerate(mix_units):
        units += [("mix", d, q)] + second[per_mix * i:per_mix * (i + 1)]
    HB = CH // COLS
    up_units = [("up", g, q) for g in range(HB) for q in range(DT // UK)]
    down_units = [("down", 0, 0), ("down", 1, 0), ("down", 0, 1), ("down", 1, 1),
                  ("down", 2, 0), ("down", 2, 1), ("down", 3, 0), ("down", 3, 1)]
    chunk_units = up_units + down_units
    UP_END = [1 + max(j for j, w in enumerate(chunk_units) if w[:2] == ("up", g)) for g in range(HB)]
    DOWN_END = [1 + max(j for j, w in enumerate(chunk_units) if w[:2] == ("down", d)) for d in range(DB)]
    MODS1 = 5
    MODS_READY = MODS1 + DT + 3
    per_up = DT // len(up_units)
    FIRST_CHUNK = len(units)
    for i, w in enumerate(up_units):
        units += [w] + [("ada", GATE2, k) for k in range(per_up * i, per_up * (i + 1))]
    units += down_units
    LATER = len(units)
    CU = len(chunk_units)
    assert CU % RAW == 0 and CU % WS == 0 and len(mix_units) % WS == 0
    MU = len(mix_units)
    ada_order = [w for w in units if w[0] == "ada"]
    weight_order = [w for w in units if w[0] in ("mix", "up", "down")]
    position = {w: u for u, w in enumerate(units[:FIRST_CHUNK])}
    position.update({("c0",) + w if w[0] in ("up", "down") else w: FIRST_CHUNK + i
                     for i, w in enumerate(units[FIRST_CHUNK:])})

    def unit_at(chunk, j):
        if isinstance(chunk, int) and chunk == 0:
            return position[("c0",) + chunk_units[j]]
        return (chunk - 1) * CU + (LATER + j)

    def slot_of(chunk, j):
        return unit_at(0, j) % RAW if isinstance(chunk, int) and chunk == 0 else (LATER + j) % RAW

    def uses_of(chunk, j):
        if isinstance(chunk, int) and chunk == 0:
            return unit_at(0, j) // RAW
        return (chunk - 1) * (CU // RAW) + (LATER + j) // RAW

    ada_v = w_ada.rearrange("(k p) n -> p k n", p=P)
    mix_v = w_mix.rearrange("(k p) n -> p k n", p=P)
    up_v = w_ffn_in.rearrange("(k p) n -> p k n", p=P)
    down_v = w_ffn_out.rearrange("(k p) n -> p k n", p=P)

    with ExitStack() as ctx:
        top = [nc.sbuf_base + (-nc.sbuf_base) % 32]

        def region(words):
            at = top[0]
            top[0] += (4 * words + 31) // 32 * 32
            assert top[0] <= nc.sbuf_usable_end
            return at

        def place(name, shape, dt, at, skip=0):
            return nc.alloc_sbuf_tensor_at(name, shape, dt, offset=at + 4 * skip)

        at_x, at_acts, at_hid, at_w = (region(TT * D), region(2 * DT * N), region(2 * HT * N),
                                       region(2 * WS * UNIT))
        at_raw, at_gate, at_acc, at_tmp = region(RAW * UNIT), region(D), region(D), region(D)
        xres = place("xres", [P, TT, D], F32, at_x)
        acts = place("acts", [P, DT, 2, N], F32R, at_acts)
        spec = place("spec", [P, DT, N], F32, at_acts, skip=DT * N)
        hid = place("hid", [P, HT, 2, N], F32R, at_hid)
        seqt = place("seqt", [P, 2, TT, N], F32R, at_hid)
        modp = place("modp", [P, 2, 2, GT, N], F32R, at_hid)
        acc_b = place("acc_b", [P, D], F32, at_hid, skip=2 * HT * N - D)
        normed = place("normed", [P, TT, D], F32, at_hid)
        wsp = place("wsp", [P, WS, 2, UK, COLS], F32R, at_w)
        xsp = place("xsp", [P, 2, 2, TT, GD], F32R, at_w)
        chant = place("chant", [P, 4, GT, GD], F32R, at_w)
        raw = place("raw", [P, RAW, UNIT], F32, at_raw)
        gate = place("gate", [P, D], F32, at_gate)
        acc_a = place("acc_a", [P, D], F32, at_acc)
        gfin = place("gfin", [P, D], F32, at_acc)
        junk = place("junk", [P, D], F32, at_tmp)
        relu = place("relu", [P, 2, COLS], F32, at_tmp)
        square = place("square", [P, 2, COLS], F32, at_tmp, skip=2 * COLS)
        gated = place("gated", [P, TT, COLS], F32, at_tmp)
        four = place("four", [P, 2, N], F32, at_tmp)
        odd = place("odd", [P, 2, HALF], F32, at_tmp, skip=2 * N)
        hmod = place("hmod", [P, 2, N], F32, at_tmp)

        def small(name, shape):
            words = int(np.prod(shape[1:]))
            return place(name, shape, F32, region(words))

        ident = small("ident", [P, P])
        ones = small("ones", [P, P])
        vecs = small("vecs", [P, P])
        vec_t = small("vec_t", [P, P])
        c_rows = small("c_rows", [DT, P])
        c_exp = small("c_exp", [P, DT])
        c_den = small("c_den", [P, DT])
        c_t = small("c_t", [P, DT])
        silu = small("silu", [P, DT])
        mods = small("mods", [P, 6, DT])
        ssq = small("ssq", [P, 3, TT])
        rms = small("rms", [P, 3, TT])
        mean = small("mean", [P, 3, TT])
        inv = small("inv", [P, 3, TT])
        brow = gate[0:1, :]

        banks = ctx.enter_context(nc.psum_tensor("banks", [P, 8, COLS], F32))

        def sem(name):
            return ctx.enter_context(nc.semaphore(name))

        const_in = sem("const_in")
        brow_in = sem("brow_in")
        x_in = [sem(f"x_in{t}") for t in range(TT)]
        raw_full = [sem(f"raw_full{s}") for s in range(RAW)]
        ones_set = sem("ones_set")
        turned = sem("turned")
        vec_ready = sem("vec_ready")
        exp_done = sem("exp_done")
        silu_step = sem("silu_step")
        silu_ready = sem("silu_ready")
        sq_done = sem("sq_done")
        mean_done = sem("mean_done")
        rms_done = sem("rms_done")
        inv_done = sem("inv_done")
        xhi_done, xlo_done = sem("xhi_done"), sem("xlo_done")
        table_ready = sem("table_ready")
        spec_sum, spec_done = sem("spec_sum"), sem("spec_done")
        gemv_step = sem("gemv_step")
        col_sum = sem("col_sum")
        mod_step = sem("mod_step")
        spec_mod = sem("spec_mod")
        modp_hi, modp_lo = sem("modp_hi"), sem("modp_lo")
        chan_sum = sem("chan_sum")
        odd_zero, odd_done = sem("odd_zero"), sem("odd_done")
        four_done, four_hi, four_lo = sem("four_done"), sem("four_hi"), sem("four_lo")
        gate_ready = sem("gate_ready")
        w_hi, w_lo, w_used = sem("w_hi"), sem("w_lo"), sem("w_used")
        y_read = sem("y_read")
        x_updated = sem("x_updated")
        norm_done = sem("norm_done")
        h2_turned = sem("h2_turned")
        hmod_done, h2_hi, h2_lo = sem("hmod_done"), sem("h2_hi"), sem("h2_lo")
        h_relu, h_square, h_hi, h_lo = sem("h_relu"), sem("h_square"), sem("h_hi"), sem("h_lo")
        gfin_in = sem("gfin_in")
        y_normed = sem("y_normed")
        stored = sem("stored")

        HALVES = 2 * HB
        Y1 = DB

        block = ctx.enter_context(nc.Block())

        @block.sync
        def _(sp):
            def unit_source(w, chunk):
                if w[0] == "seq":
                    return seq_table[w[1]].rearrange("(t p) n -> p t n", p=P)
                if w[0] == "chan":
                    return chan_table[w[1]].rearrange("(t p) n -> p t n", p=P)
                if w[0] == "ada":
                    return ada_v[:, w[2], w[1] * D:(w[1] + 1) * D]
                if w[0] == "mix":
                    return mix_v[:, UK * w[2]:UK * (w[2] + 1), COLS * w[1]:COLS * (w[1] + 1)]
                if w[0] == "up":
                    return up_v[:, UK * w[2]:UK * (w[2] + 1),
                                bass.ds(chunk * CH + COLS * w[1], COLS)]
                return down_v[:, bass.ds(chunk * HT + UK * w[2], UK), COLS * w[1]:COLS * (w[1] + 1)]

            def consumed(w):
                if w[0] == "ada":
                    return gemv_step, ada_order.index(w) + 1
                if w[0] in ("seq", "chan"):
                    return table_ready, (0 if w[0] == "seq" else 2) + w[1] + 1
                return w_lo, weight_order.index(w) + 1

            def load(w, slot, chunk=0):
                src = unit_source(w, chunk)
                dst = raw[:, slot, :]
                if len(src.shape) == 3:
                    dst = dst.rearrange("p (a n) -> p a n", a=src.shape[1])
                sp.dma_start(dst, src).then_inc(raw_full[slot], 16)

            for t in range(TT):
                sp.dma_start(xres[:, t, :], x[t * P:(t + 1) * P, :]).then_inc(x_in[t], 16)
            for u, w in enumerate(units):
                if u >= RAW:
                    sp.wait_ge(*consumed(units[u - RAW]))
                load(w, u % RAW)
            with sp.Fori(1, CHUNKS) as chunk:
                for j, w in enumerate(chunk_units):
                    sp.wait_ge(w_lo, chunk * CU + (MU + j - RAW + 1))
                    load(w, slot_of(chunk, j), chunk)

        @block.gpsimd
        def _(pool):
            pool.dma_start(brow, bias_rows[0:1, :]).then_inc(brow_in, 16)
            pool.wait_ge(x_updated, DB)
            pool.dma_start(brow, bias_rows[1:2, :]).then_inc(brow_in, 16)
            pool.wait_ge(col_sum, 6)
            pool.dma_start(gfin[:, :], g_final.to_broadcast([P, D])).then_inc(gfin_in, 16)

        @block.scalar
        def _(act):
            act.dma_start(ident[:, :], identity).then_inc(const_in, 16)
            act.dma_start(vecs[:, :], vectors).then_inc(const_in, 16)
            act.dma_start(c_rows[:, :], c).then_inc(const_in, 16)
            act.wait_ge(vec_ready, 1)
            nc.scalar.activation(c_exp[:, :], c_t[:, :], ACT.Exp, scale=-1.0).then_inc(exp_done, 1)

            def root(stage):
                act.wait_ge(mean_done, stage + 1)
                nc.scalar.activation(rms[:, stage, :], mean[:, stage, :], ACT.Sqrt).then_inc(rms_done, 1)

            for t in range(TT):
                act.wait_ge(x_in[t], 16)
                if t >= 1:
                    act.wait_ge(sq_done, t)
                nc.scalar.activation(junk[:, :], xres[:, t, :], ACT.Square,
                                     accum_out=ssq[:, 0, t:t + 1]).then_inc(sq_done, 1)
            root(0)
            act.wait_ge(inv_done, 1)
            def evacuate_spec(d):
                act.wait_ge(spec_sum, d + 1)
                nc.scalar.activation(spec[:, d, :], banks[:, d % 4, :], ACT.Copy).then_inc(spec_done, 1)

            for q in range(GROUPS):
                if q >= 2:
                    act.wait_ge(spec_sum, GT * (q - 1))
                for t in range(TT):
                    nc.scalar.activation(xsp[:, q % 2, 0, t, :], xres[:, t, q * GD:(q + 1) * GD], ACT.Copy,
                                         scale=inv[:, 0, t:t + 1]).then_inc(xhi_done, 1)
                if q >= 1:
                    for d in range(GT * (q - 1), GT * q):
                        evacuate_spec(d)
            for d in range(GT * (GROUPS - 1), DT):
                evacuate_spec(d)

            def spec_high(g):
                act.wait_ge(spec_mod, g + 1)
                if g >= 2:
                    act.wait_ge(chan_sum, GT * (g - 1))
                nc.scalar.activation(modp[:, g % 2, 0, :, :], spec[:, GT * g:GT * (g + 1), :],
                                     ACT.Copy).then_inc(modp_hi, 1)

            spec_high(0)
            spec_high(1)
            for k in range(DT):
                act.wait_ge(chan_sum, k + 1)
                if k == 0:
                    act.wait_ge(odd_zero, 1)
                if k >= 2:
                    act.wait_ge(four_done, k - 1)
                nc.scalar.activation(odd[:, k % 2, 1:HALF], banks[:, 2 * (k % 2) + 1, 1:HALF],
                                     ACT.Copy).then_inc(odd_done, 1)
                act.wait_ge(four_done, k + 1)
                nc.scalar.activation(acts[:, k, 0, :], four[:, k % 2, :], ACT.Copy).then_inc(four_hi, 1)
                if k % GT == GT - 1 and k // GT + 2 < GROUPS:
                    spec_high(k // GT + 2)

            def weight_high(n, slot, uses, ws, used):
                act.wait_ge(raw_full[slot], (uses + 1) * 16)
                if used is not None:
                    act.wait_ge(w_used, used)
                nc.scalar.activation(wsp[:, ws, 0, :, :], raw[:, slot, :].rearrange("p (a n) -> p a n", a=UK),
                                     ACT.Copy).then_inc(w_hi, 1)

            act.wait_ge(chan_sum, DT)
            for n, w in enumerate(mix_units):
                u = position[("mix",) + w]
                weight_high(n, u % RAW, u // RAW, n % WS, n - WS + 1 if n >= WS else None)
                if n == 1:
                    act.wait_ge(col_sum, 3)
                    nc.scalar.activation(gate[:, :].rearrange("p (a n) -> p a n", a=DB),
                                         banks[:, 4:8, :], ACT.Copy).then_inc(gate_ready, 1)
            def chunk_high(chunk, j):
                weight_high(None, slot_of(chunk, j), uses_of(chunk, j), j % WS, MU + CU * chunk + j - WS + 1)

            chunk_high(0, 0)
            chunk_high(0, 1)
            for t in range(TT):
                act.wait_ge(x_updated, DB)
                act.wait_ge(sq_done, TT + t)
                nc.scalar.activation(junk[:, :], xres[:, t, :], ACT.Square,
                                     accum_out=ssq[:, 1, t:t + 1]).then_inc(sq_done, 1)
            root(1)
            act.wait_ge(mod_step, MODS_READY)
            for k in range(DT):
                act.wait_ge(h2_turned, k + 1)
                if k >= 2:
                    act.wait_ge(h2_lo, k - 1)
                nc.scalar.activation(hmod[:, k % 2, :], banks[:, 4 + k % 4, :], ACT.Identity,
                                     scale=mods[:, SCALE2, k:k + 1],
                                     bias=mods[:, SHIFT2, k:k + 1]).then_inc(hmod_done, 1)
                act.wait_ge(hmod_done, k + 1)
                nc.scalar.activation(acts[:, k, 0, :], hmod[:, k % 2, :], ACT.Copy).then_inc(h2_hi, 1)

            def hidden_relu(chunk, g, half):
                h = HALVES * chunk + 2 * g + half
                act.wait_ge(w_used, CU * chunk + (MU + UP_END[g]))
                if half == 0 and g == 0:
                    act.wait_ge(x_updated, Y1 + DB * chunk)
                if half == 0:
                    act.wait_ge(h2_lo, DT)
                if not isinstance(h, int) or h >= 1:
                    act.wait_ge(h_square, h)
                b = 4 * (g % 2) + 2 * half
                nc.scalar.activation(relu[:, :, :], banks[:, b:b + 2, :], ACT.Relu).then_inc(h_relu, 1)

            def hidden_high(chunk, g, half):
                h = HALVES * chunk + 2 * g + half
                act.wait_ge(h_square, h + 1)
                t = 4 * g + 2 * half
                nc.scalar.activation(hid[:, t:t + 2, 0, :], square[:, :, :], ACT.Copy).then_inc(h_hi, 1)

            def chunk_body(chunk):
                for j in range(CU):
                    if not (isinstance(chunk, int) and chunk == 0 and j < 2):
                        if j == DT // UK + 1 or j == 2 * (DT // UK) + 1:
                            if j == 2 * (DT // UK) + 1 and isinstance(chunk, int) and chunk == 0:
                                act.wait_ge(col_sum, 6)
                                nc.scalar.activation(gate[:, :].rearrange("p (a n) -> p a n", a=DB),
                                                     banks[:, 0:4, :], ACT.Copy).then_inc(gate_ready, 1)
                            hidden_relu(chunk, j // (DT // UK) - 1, 0)
                        chunk_high(chunk, j)
                        if j == DT // UK + 1 or j == 2 * (DT // UK) + 1:
                            g = j // (DT // UK) - 1
                            hidden_relu(chunk, g, 1)
                            hidden_high(chunk, g, 0)
                            hidden_high(chunk, g, 1)

            chunk_body(0)
            with act.Fori(1, CHUNKS) as chunk:
                chunk_body(chunk)
            for t in range(TT):
                act.wait_ge(x_updated, Y1 + DB * CHUNKS)
                act.wait_ge(sq_done, 2 * TT + t)
                nc.scalar.activation(junk[:, :], xres[:, t, :], ACT.Square,
                                     accum_out=ssq[:, 2, t:t + 1]).then_inc(sq_done, 1)
            root(2)
            for t in range(TT):
                act.wait_ge(y_normed, t + 1)
                act.dma_start(out[t * P:(t + 1) * P, :], xres[:, t, :]).then_inc(stored, 16)
            act.wait_ge(stored, 16 * TT)

        @block.vector
        def _(dve):
            nc.vector.memset(ones[:, :], 1.0).then_inc(ones_set, 1)
            dve.wait_ge(turned, 1)
            nc.vector.tensor_copy(c_t[:, :], banks[:, 1, 0:DT]).then_inc(vec_ready, 1)
            nc.vector.tensor_copy(vec_t[:, :], banks[:, 0, 0:P]).then_inc(vec_ready, 1)
            dve.wait_ge(exp_done, 1)
            nc.vector.tensor_scalar(c_den[:, :], c_exp[:, :], 1.0, None, ALU.add).then_inc(silu_step, 1)
            dve.wait_ge(silu_step, 1)
            nc.vector.reciprocal(c_exp[:, :], c_den[:, :]).then_inc(silu_step, 1)
            dve.wait_ge(silu_step, 2)
            nc.vector.tensor_tensor(silu[:, :], c_t[:, :], c_exp[:, :], ALU.mult).then_inc(silu_ready, 1)

            def inverse(stage):
                dve.wait_ge(sq_done, (stage + 1) * TT)
                nc.vector.tensor_scalar(mean[:, stage, :], ssq[:, stage, :], 1.0 / D, EPS,
                                        ALU.mult, ALU.add).then_inc(mean_done, 1)
                dve.wait_ge(rms_done, stage + 1)
                nc.vector.reciprocal(inv[:, stage, :], rms[:, stage, :]).then_inc(inv_done, 1)
                dve.wait_ge(inv_done, stage + 1)

            steps = [0]

            def gemv(j, k):
                u = position[("ada", j, k)]
                s = u % RAW
                acc = acc_a if j in (SCALE1, GATE1, SHIFT2, GATE2) else acc_b
                if steps[0] == 0:
                    dve.wait_ge(silu_ready, 1)
                if k == 0 and j in (GATE1, SHIFT2, GATE2):
                    dve.wait_ge(col_sum, {GATE1: 1, SHIFT2: 3, GATE2: 4}[j])
                if k == 0 and j == SCALE2:
                    dve.wait_ge(chan_sum, DT)
                dve.wait_ge(raw_full[s], (u // RAW + 1) * 16)
                if k == 0:
                    ins = nc.vector.tensor_scalar(acc[:, :], raw[:, s, :], silu[:, 0:1], None, ALU.mult)
                else:
                    dve.wait_ge(gemv_step, steps[0])
                    ins = nc.vector.scalar_tensor_tensor(acc[:, :], raw[:, s, :], silu[:, k:k + 1], acc[:, :],
                                                         ALU.mult, ALU.add)
                ins.then_inc(gemv_step, 1)
                steps[0] += 1

            def table(dst, w):
                u = position[w]
                dve.wait_ge(raw_full[u % RAW], (u // RAW + 1) * 16)
                nc.vector.tensor_copy(dst, raw[:, u % RAW, :].rearrange("p (a n) -> p a n", a=UK))\
                    .then_inc(table_ready, 1)

            def x_low(q):
                for t in range(TT):
                    dve.wait_ge(xhi_done, TT * q + t + 1)
                    nc.vector.scalar_tensor_tensor(
                        xsp[:, q % 2, 1, t, :], xres[:, t, q * GD:(q + 1) * GD], inv[:, 0, t:t + 1],
                        xsp[:, q % 2, 0, t, :].bitcast(F32), ALU.mult, ALU.subtract).then_inc(xlo_done, 1)

            for i in range(2):
                table(seqt[:, i, :, :], ("seq", i))
            gemv(SCALE1, 0)
            inverse(0)
            for q in range(GROUPS):
                x_low(q)
                for k in range(1 + 4 * q, min(5 + 4 * q, DT)):
                    gemv(SCALE1, k)
            dve.wait_ge(spec_sum, DT)
            for i in range(4):
                table(chant[:, i, :, :], ("chan", i))
            for k in range(DT):
                gemv(SHIFT1, k)

            def add_bias(j, bank, col):
                nc.vector.tensor_tensor(mods[:, j, :], banks[:, bank, col:col + DT],
                                        vec_t[:, j * DT:(j + 1) * DT], ALU.add).then_inc(mod_step, 1)

            def times_gain(j, gain):
                nc.vector.scalar_tensor_tensor(mods[:, j, :], mods[:, j, :], 1.0, gain, ALU.add,
                                               ALU.mult).then_inc(mod_step, 1)

            dve.wait_ge(col_sum, 2)
            dve.wait_ge(vec_ready, 2)
            add_bias(SCALE1, 4, 0)
            add_bias(SHIFT1, 5, 0)
            dve.wait_ge(mod_step, 2)
            times_gain(SCALE1, vec_t[:, 6 * DT:7 * DT])
            dve.wait_ge(mod_step, 3)
            nc.vector.tensor_scalar(mods[:, SCALE1, :], mods[:, SCALE1, :], NORM, None, ALU.mult)\
                .then_inc(mod_step, 1)
            nc.vector.tensor_scalar(mods[:, SHIFT1, :], mods[:, SHIFT1, :], N * NORM, None, ALU.mult)\
                .then_inc(mod_step, 1)
            dve.wait_ge(mod_step, MODS1)
            dve.wait_ge(spec_done, DT)
            nc.vector.memset(odd[:, :, 0:1], 0.0).then_inc(odd_zero, 1)

            scaled = [0]

            def modulate(g):
                for d in range(GT * g, GT * (g + 1)):
                    nc.vector.tensor_scalar(spec[:, d, :], spec[:, d, :], mods[:, SCALE1, d:d + 1], None,
                                            ALU.mult).then_inc(mod_step, 1)
                    scaled[0] += 1
                dve.wait_ge(mod_step, MODS1 + scaled[0])
                zero = spec[:, GT * g:GT * (g + 1), 0:1].rearrange("p a b -> p (a b)")
                nc.vector.tensor_tensor(zero, zero, mods[:, SHIFT1, GT * g:GT * (g + 1)], ALU.add)\
                    .then_inc(spec_mod, 1)

            def spec_low(g):
                dve.wait_ge(modp_hi, g + 1)
                nc.vector.tensor_tensor(modp[:, g % 2, 1, :, :], spec[:, GT * g:GT * (g + 1), :],
                                        modp[:, g % 2, 0, :, :].bitcast(F32), ALU.subtract)\
                    .then_inc(modp_lo, 1)

            def four_tile(k):
                dve.wait_ge(odd_done, k + 1)
                even = banks[:, 2 * (k % 2), :]
                if k >= 2:
                    dve.wait_ge(four_lo, k - 1)
                    dve.wait_ge(four_hi, k - 1)
                nc.vector.tensor_tensor(four[:, k % 2, 0:HALF], even[:, 0:HALF], odd[:, k % 2, :],
                                        ALU.subtract)
                nc.vector.tensor_tensor(four[:, k % 2, N - 1:HALF:-1], even[:, 1:HALF],
                                        odd[:, k % 2, 1:HALF], ALU.add)
                nc.vector.tensor_copy(four[:, k % 2, HALF:HALF + 1], even[:, HALF:HALF + 1])\
                    .then_inc(four_done, 1)
                dve.wait_ge(four_hi, k + 1)
                nc.vector.tensor_tensor(acts[:, k, 1, :], four[:, k % 2, :], acts[:, k, 0, :].bitcast(F32),
                                        ALU.subtract).then_inc(four_lo, 1)

            modulate(0)
            modulate(1)
            spec_low(0)
            modulate(2)
            modulate(3)
            spec_low(1)
            for k in range(DT):
                four_tile(k)
                gemv(GATE1, k)
                if k % GT == GT - 1 and k // GT + 2 < GROUPS:
                    spec_low(k // GT + 2)

            def weight_low(slot, ws, n):
                dve.wait_ge(w_hi, n + 1)
                nc.vector.tensor_tensor(wsp[:, ws, 1, :, :],
                                        raw[:, slot, :].rearrange("p (a n) -> p a n", a=UK),
                                        wsp[:, ws, 0, :, :].bitcast(F32), ALU.subtract).then_inc(w_lo, 1)

            def update_x(y, b, d, gates, done):
                dve.wait_ge(w_used, done)
                dve.wait_ge(gate_ready, gates)
                if not isinstance(y, int) or y >= 1:
                    dve.wait_ge(x_updated, y)
                cols = slice(COLS * d, COLS * (d + 1))
                nc.vector.tensor_tensor(gated[:, :, :], banks[:, b:b + 4, :],
                                        gate[:, cols].unsqueeze(1).to_broadcast([P, TT, COLS]),
                                        ALU.mult).then_inc(y_read, 1)
                dve.wait_ge(y_read, y + 1)
                nc.vector.tensor_tensor(xres[:, :, cols], xres[:, :, cols], gated[:, :, :],
                                        ALU.add).then_inc(x_updated, 1)

            dve.wait_ge(four_lo, DT)
            for n, w in enumerate(mix_units):
                u = position[("mix",) + w]
                weight_low(u % RAW, n % WS, n)
                for j, k in [s[1:] for s in second[per_mix * n:per_mix * (n + 1)]]:
                    gemv(j, k)
                if n % (DT // UK) == 1 and n > DT // UK:
                    y = n // (DT // UK) - 1
                    update_x(y, 4 * (y % 2), y, 1, (y + 1) * (DT // UK))
            weight_low(slot_of(0, 0), 0, MU)
            weight_low(slot_of(0, 1), 1, MU + 1)
            update_x(DB - 1, 4, DB - 1, 1, MU)
            dve.wait_ge(col_sum, 5)
            add_bias(SHIFT2, 0, 0)
            add_bias(SCALE2, 0, DT)
            dve.wait_ge(mod_step, MODS_READY - 1)
            times_gain(SCALE2, vec_t[:, 7 * DT:8 * DT])
            dve.wait_ge(x_updated, DB)
            inverse(1)
            for t in range(TT):
                nc.vector.tensor_scalar(normed[:, t, :], xres[:, t, :], inv[:, 1, t:t + 1], None, ALU.mult)\
                    .then_inc(norm_done, 1)
            for k in range(DT):
                dve.wait_ge(h2_hi, k + 1)
                nc.vector.tensor_tensor(acts[:, k, 1, :], hmod[:, k % 2, :], acts[:, k, 0, :].bitcast(F32),
                                        ALU.subtract).then_inc(h2_lo, 1)

            def hidden_square(chunk, g, half):
                h = HALVES * chunk + 2 * g + half
                dve.wait_ge(h_relu, h + 1)
                if not isinstance(h, int) or h >= 1:
                    dve.wait_ge(h_lo, h)
                nc.vector.tensor_tensor(square[:, :, :], relu[:, :, :], relu[:, :, :], ALU.mult)\
                    .then_inc(h_square, 1)

            def hidden_low(chunk, g, half):
                h = HALVES * chunk + 2 * g + half
                dve.wait_ge(h_hi, h + 1)
                t = 4 * g + 2 * half
                nc.vector.tensor_tensor(hid[:, t:t + 2, 1, :], square[:, :, :], hid[:, t:t + 2, 0, :].bitcast(F32),
                                        ALU.subtract).then_inc(h_lo, 1)

            def chunk_body(chunk):
                first = isinstance(chunk, int) and chunk == 0
                for j in range(CU):
                    hidden = j == DT // UK + 1 or j == 2 * (DT // UK) + 1
                    g = j // (DT // UK) - 1
                    if hidden:
                        hidden_square(chunk, g, 0)
                    if not (first and j < 2):
                        weight_low(slot_of(chunk, j), j % WS, MU + CU * chunk + j)
                    if hidden:
                        hidden_low(chunk, g, 0)
                        hidden_square(chunk, g, 1)
                        hidden_low(chunk, g, 1)
                    if first and j < len(up_units):
                        for k in range(per_up * j, per_up * (j + 1)):
                            gemv(GATE2, k)
                    if j == 1 and not first:
                        update_x(DB * chunk + (Y1 - 1), 4, DB - 1, 2, CU * chunk + MU)
                    for d in range(DB - 1):
                        if j == DOWN_END[d] + 1:
                            update_x(DB * chunk + (Y1 + d), 4 * (d % 2), d, 2, CU * chunk + (MU + DOWN_END[d]))

            chunk_body(0)
            with dve.Fori(1, CHUNKS) as chunk:
                chunk_body(chunk)
            update_x(Y1 + DB * CHUNKS - 1, 4, DB - 1, 2, MU + CU * CHUNKS)
            inverse(2)
            dve.wait_ge(gfin_in, 16)
            for t in range(TT):
                nc.vector.scalar_tensor_tensor(xres[:, t, :], xres[:, t, :], inv[:, 2, t:t + 1], gfin[:, :],
                                               ALU.mult, ALU.mult).then_inc(y_normed, 1)

        @block.tensor
        def _(pe):
            def product(bank, w_hi_ap, w_lo_ap, m_hi, m_lo, first, last):
                nc.tensor.matmul(bank, w_hi_ap, m_hi, start=first, stop=False)
                nc.tensor.matmul(bank, w_hi_ap, m_lo, start=False, stop=False)
                return nc.tensor.matmul(bank, w_lo_ap, m_hi, start=False, stop=last)

            pe.wait_ge(const_in, 48)
            nc.tensor.transpose(banks[:, 0, 0:P], vecs[:, :], ident[:, :])
            nc.tensor.transpose(banks[:, 1, 0:DT], c_rows[:, :], ident[0:DT, 0:DT]).then_inc(turned, 1)
            pe.wait_ge(vec_ready, 2)
            pe.wait_ge(table_ready, 2)
            for q in range(GROUPS):
                pe.wait_ge(xlo_done, TT * (q + 1))
                for d in range(GT * q, GT * (q + 1)):
                    if d >= 4:
                        pe.wait_ge(spec_done, d - 3)
                    cols = slice(P * (d % GT), P * (d % GT + 1))
                    for t in range(TT):
                        mm = product(banks[:, d % 4, :], xsp[:, q % 2, 0, t, cols], xsp[:, q % 2, 1, t, cols],
                                     seqt[:, 0, t, :], seqt[:, 1, t, :], t == 0, t == TT - 1)
                    mm.then_inc(spec_sum, 1)

            def column_sums(acc, bank, col):
                for d in range(DT):
                    mm = nc.tensor.matmul(banks[:, bank, col + d:col + d + 1], acc[:, P * d:P * (d + 1)],
                                          ones[:, 0:1], start=(d == 0 and col == 0), stop=True, skip_group_check=True)
                mm.then_inc(col_sum, 1)

            def row_sums(acc, bank, rows):
                pe.wait_ge(brow_in, 16 * rows)
                for d in range(DB):
                    cols = slice(COLS * d, COLS * (d + 1))
                    nc.tensor.matmul(banks[:, bank + d, :], ones[0:1, :], brow[0:1, cols], start=True, stop=False)
                    mm = nc.tensor.matmul(banks[:, bank + d, :], ones[:, :], acc[:, cols], start=False, stop=True)
                mm.then_inc(col_sum, 1)

            pe.wait_ge(ones_set, 1)
            pe.wait_ge(gemv_step, DT)
            column_sums(acc_a, 4, 0)
            pe.wait_ge(gemv_step, 2 * DT)
            column_sums(acc_b, 5, 0)

            pe.wait_ge(table_ready, 6)
            for k in range(DT):
                g, kt = k // GT, k % GT
                pe.wait_ge(modp_lo, g + 1)
                if k >= 2:
                    pe.wait_ge(four_done, k - 1)
                else:
                    pe.wait_ge(spec_done, DT)
                cols = slice(P * kt, P * (kt + 1))
                even, odd_b = banks[:, 2 * (k % 2), 0:HALF + 2], banks[:, 2 * (k % 2) + 1, 0:HALF]
                for d in range(GT):
                    product(even, chant[:, 0, d, cols], chant[:, 1, d, cols], modp[:, g % 2, 0, d, 0:HALF + 2],
                            modp[:, g % 2, 1, d, 0:HALF + 2], d == 0, d == GT - 1)
                for d in range(GT):
                    mm = product(odd_b, chant[:, 2, d, cols], chant[:, 3, d, cols], modp[:, g % 2, 0, d, HALF:],
                                 modp[:, g % 2, 1, d, HALF:], d == 0, d == GT - 1)
                mm.then_inc(chan_sum, 1)

            def token_unit(b, ws, n, left, q, k_tiles):
                pe.wait_ge(w_lo, n + 1)
                for kk in range(UK):
                    k = UK * q + kk
                    for t in range(TT):
                        tok = slice(P * t, P * (t + 1))
                        mm = product(banks[:, b + t, :], left[:, k, 0, tok], left[:, k, 1, tok],
                                     wsp[:, ws, 0, kk, :], wsp[:, ws, 1, kk, :], k == 0, k == k_tiles - 1)
                mm.then_inc(w_used, 1)

            pe.wait_ge(four_lo, DT)
            for n, (d, q) in enumerate(mix_units):
                if q == 0:
                    if d == 1:
                        pe.wait_ge(gate_ready, 1)
                    if d >= 2:
                        pe.wait_ge(y_read, d - 1)
                token_unit(4 * (d % 2), n % WS, n, acts, q, DT)
                if n == 0:
                    pe.wait_ge(gemv_step, 3 * DT)
                    row_sums(acc_a, 4, 1)
            pe.wait_ge(y_read, DB - 1)
            pe.wait_ge(gemv_step, 5 * DT)
            column_sums(acc_a, 0, 0)
            column_sums(acc_b, 0, DT)
            pe.wait_ge(norm_done, TT)
            for k in range(DT):
                if k >= 4:
                    pe.wait_ge(hmod_done, k - 3)
                for t in range(TT):
                    mm = nc.tensor.transpose(banks[:, 4 + k % 4, P * t:P * (t + 1)],
                                             normed[:, t, P * k:P * (k + 1)], ident[:, :])
                mm.then_inc(h2_turned, 1)

            def chunk_body(chunk):
                first = isinstance(chunk, int) and chunk == 0
                for j, (what, a, q) in enumerate(chunk_units):
                    n = MU + CU * chunk + j
                    b = 4 * (a % 2)
                    if what == "up":
                        if q == 0:
                            pe.wait_ge(y_read, Y1 + DB * chunk - 1 + a)
                            if first and a == 0:
                                pe.wait_ge(mod_step, MODS_READY)
                        pe.wait_ge(w_lo, n + 1)
                        for kk in range(UK):
                            k = UK * q + kk
                            if first and a == 0:
                                pe.wait_ge(h2_lo, k + 1)
                            for f in range(4):
                                cols = slice(P * f, P * (f + 1))
                                mm = product(banks[:, b + f, :], wsp[:, j % WS, 0, kk, cols],
                                             wsp[:, j % WS, 1, kk, cols], acts[:, k, 0, :], acts[:, k, 1, :],
                                             k == 0, k == DT - 1)
                        mm.then_inc(w_used, 1)
                        if first and j == len(up_units) - 1:
                            pe.wait_ge(h_relu, 2)
                            pe.wait_ge(gemv_step, 6 * DT)
                            row_sums(acc_a, 0, 2)
                            pe.wait_ge(gate_ready, 2)
                    else:
                        if q == 0:
                            if a < 2:
                                pe.wait_ge(h_relu, HALVES * chunk + 2 * (a + 1))
                            else:
                                pe.wait_ge(y_read, Y1 + DB * chunk + a - 1)
                        pe.wait_ge(h_lo, HALVES * chunk + 2 * (q + 1))
                        token_unit(b, j % WS, n, hid, q, HT)

            chunk_body(0)
            with pe.Fori(1, CHUNKS) as chunk:
                chunk_body(chunk)


INPUTS = ("x", "c", "w_ada", "vectors", "bias_rows", "g_final", "w_mix", "w_ffn_in", "w_ffn_out",
          "seq_table", "chan_table", "identity")


def split12(a):
    hi = a.astype(np.float32).view(np.uint32)
    hi = ((hi + np.uint32(0x7FF) + ((hi >> 12) & 1)) & np.uint32(0xFFFFF000)).view(np.float32)
    return hi, (a - hi.astype(np.float64)).astype(np.float32)


def fourier_tables(n):
    a = np.arange(n)
    angle = 2 * np.pi * (np.outer(a, a) % n) / n
    cos, sin = np.cos(angle), np.sin(angle)
    half = n // 2
    seq = np.concatenate([cos[:, :half + 1], sin[:, 1:half]], axis=1)
    return np.stack(split12(seq)), np.stack(split12(cos) + split12(sin))


def kernel(**inputs):
    import concourse.bacc as bacc
    from concourse.bass_utils import run_bass_kernel_spmd

    a = {k: np.ascontiguousarray(np.asarray(v)) for k, v in inputs.items()}
    n, d = a["x"].shape[1:]
    b_ada = a["b_ada"][0]
    seq_table, chan_table = fourier_tables(n)
    data = {
        "x": a["x"][0], "c": a["c"].reshape(d // 128, 128), "w_ada": a["w_ada"][0],
        "vectors": np.concatenate([b_ada, a["g_norm_mix"][0], a["g_norm_ffn"][0]]).reshape(-1, 128),
        "bias_rows": np.stack([b_ada[2 * d:3 * d], b_ada[5 * d:6 * d]]),
        "g_final": a["g_final"].reshape(1, d), "w_mix": a["fno_w_out"][0],
        "w_ffn_in": a["w_ffn_in"][0], "w_ffn_out": a["w_ffn_out"][0],
        "seq_table": seq_table, "chan_table": chan_table, "identity": np.eye(128, dtype=np.float32),
    }
    data = {f"in_{k}": np.ascontiguousarray(data[k]) for k in INPUTS}
    nc = bacc.Bacc("TRN2", target_bir_lowering=False, num_devices=1, dynamic_dma_scratch_size=1024)
    aps = [nc.dram_tensor(k, v.shape, mybir.dt.from_np(v.dtype), kind="ExternalInput").ap()
           for k, v in data.items()]
    out = nc.dram_tensor("out", (n, d), mybir.dt.float32, kind="ExternalOutput").ap()
    fourier_ffn_block(nc, *aps, out)
    result = run_bass_kernel_spmd(nc, [data], core_ids=[0])
    return result.results[0]["out"].reshape(1, n, d)
```

```python
import math
from contextlib import ExitStack

import numpy as np

import concourse.bass as bass
from concourse import mybir


def fourier_ffn_block(nc, x, c, w_ada, vectors, bias_rows, g_final, w_mix, w_ffn_in, w_ffn_out,
                      seq_table, cos_table, sin_table, identity, out):
    F32, F32R = mybir.dt.float32, mybir.dt.float32r
    ALU, ACT = mybir.AluOpType, mybir.ActivationFunctionType

    P = 128
    N, D = x.shape
    FF = w_ffn_in.shape[1]
    TT = N // P
    DT = D // P
    GROUPS = 4
    GD = D // GROUPS
    GT = GD // P
    FT = 3
    HALF = N // 2
    COLS = 512
    UK = 4
    UNIT = UK * COLS
    DB = D // COLS
    CH = 1024
    CHUNKS = FF // CH
    HT = CH // P
    RAW = 4
    WS = 2
    EPS = 1e-6
    NORM = 1.0 / math.sqrt(N * GD)
    assert N == GD == COLS and D == UNIT

    SHARE = 4
    SHIFT1, SCALE1, GATE1, SHIFT2, SCALE2, GATE2 = range(6)
    units = [("seq",)] + [("ada", SCALE1, k) for k in range(DT)]
    units += [("cos",), ("sin",)] + [("ada", SHIFT1, k) for k in range(DT)]
    mix_units = [(d, q) for d in range(DB) for q in range(GROUPS)]
    others = [("ada", j, k) for j in (GATE1, SHIFT2, SCALE2) for k in range(DT)]
    between = [3, 3, 2] * 5 + [len(others)]
    runs = []
    for i, w in enumerate(mix_units):
        runs.append(others[:between[i]])
        others = others[between[i]:]
        units += [("mix",) + w] + runs[-1]
    HB = CH // COLS
    up_units = [("up", g, q) for g in range(HB) for q in range(DT // UK)]
    down_units = [("down", 0, 0), ("down", 1, 0), ("down", 0, 1), ("down", 1, 1),
                  ("down", 2, 0), ("down", 2, 1), ("down", 3, 0), ("down", 3, 1)]
    chunk_units = up_units + down_units
    UP_END = [1 + max(j for j, w in enumerate(chunk_units) if w[:2] == ("up", g)) for g in range(HB)]
    DOWN_END = [1 + max(j for j, w in enumerate(chunk_units) if w[:2] == ("down", d)) for d in range(DB)]
    LAST_SCALE = DT - SHARE
    MODS1 = 5
    MODS_READY = MODS1 + 3
    per_up = DT // len(up_units)
    FIRST_CHUNK = len(units)
    for i, w in enumerate(up_units):
        units += [w] + [("ada", GATE2, k) for k in range(per_up * i, per_up * (i + 1))]
    units += down_units
    LATER = len(units)
    CU = len(chunk_units)
    assert CU % RAW == 0 and CU % WS == 0 and len(mix_units) % WS == 0
    MU = len(mix_units)
    GATE1_AT = 6
    UPDATED = [8, 9, 13]
    pe_order = [("ada", SCALE1, k) for k in range(DT) if k % SHARE == SHARE - 1]
    pe_order += [("ada", SHIFT1, k) for k in range(DT)]
    ada_order = [w for w in units if w[0] == "ada" and w not in pe_order]
    SCALE1_STEPS = sum(w[1] == SCALE1 for w in ada_order)
    table_order = [("seq",), ("cos",), ("sin",)]
    weight_order = [w for w in units if w[0] in ("mix", "up", "down")]
    position = {w: u for u, w in enumerate(units[:FIRST_CHUNK])}
    position.update({("c0",) + w if w[0] in ("up", "down") else w: FIRST_CHUNK + i
                     for i, w in enumerate(units[FIRST_CHUNK:])})

    def unit_at(chunk, j):
        if isinstance(chunk, int) and chunk == 0:
            return position[("c0",) + chunk_units[j]]
        return (chunk - 1) * CU + (LATER + j)

    def slot_of(chunk, j):
        return unit_at(0, j) % RAW if isinstance(chunk, int) and chunk == 0 else (LATER + j) % RAW

    fills = [0] * RAW
    filled = []
    for u, w in enumerate(units):
        fills[u % RAW] += 16
        filled.append(fills[u % RAW])

    def full_at(chunk, j):
        if isinstance(chunk, int) and chunk == 0:
            return filled[unit_at(0, j)]
        return (chunk - 1) * (16 * CU // RAW) + (fills[(LATER + j) % RAW] + 16 * (j // RAW + 1))

    ada_v = w_ada.rearrange("(k p) n -> p k n", p=P)
    mix_v = w_mix.rearrange("(k p) n -> p k n", p=P)
    up_v = w_ffn_in.rearrange("(k p) n -> p k n", p=P)
    down_v = w_ffn_out.rearrange("(k p) n -> p k n", p=P)

    with ExitStack() as ctx:
        top = [nc.sbuf_base + (-nc.sbuf_base) % 32]

        def region(words):
            at = top[0]
            top[0] += (4 * words + 31) // 32 * 32
            assert top[0] <= nc.sbuf_usable_end
            return at

        def place(name, shape, dt, at, skip=0):
            return nc.alloc_sbuf_tensor_at(name, shape, dt, offset=at + 4 * skip)

        at_x, at_acts, at_hid, at_w = (region(TT * D), region(2 * DT * N), region(2 * HT * N),
                                       region(2 * WS * UNIT))
        at_raw, at_gate, at_acc, at_tmp = region(RAW * UNIT), region(D), region(D), region(D)
        xres = place("xres", [P, TT, D], F32, at_x)
        acts = place("acts", [P, DT, 2, N], F32R, at_acts)
        fo = place("fo", [P, DT, 2, N], F32R, at_acts)
        spec = place("spec", [P, DT, N], F32, at_acts, skip=DT * N)
        hid = place("hid", [P, HT, 2, N], F32R, at_hid)
        seqt = place("seqt", [P, 2, TT, N], F32R, at_hid)
        modp = place("modp", [P, 2, 2, GT, N], F32R, at_hid)
        acc_b = place("acc_b", [P, D], F32, at_hid, skip=2 * HT * N - D)
        diag = place("diag", [P, TT, P], F32, at_hid)
        wsp = place("wsp", [P, WS, 2, UK, COLS], F32R, at_w)
        xsp = place("xsp", [P, 2, 2, TT, GD], F32R, at_w)
        cost = place("cost", [P, 2, GT, 3 * P], F32R, at_w)
        sint = place("sint", [P, 2, GT, 2 * P], F32R, at_gate)
        raw = place("raw", [P, RAW, UNIT], F32, at_raw)
        gate = place("gate", [P, D], F32, at_gate)
        acc_a = place("acc_a", [P, D], F32, at_acc)
        acc_s = place("acc_s", [P, D], F32, at_gate)
        gfin = place("gfin", [P, D], F32, at_acc)
        gained = place("gained", [P, TT, D], F32, at_acts)
        junk = place("junk", [P, D], F32, at_tmp)
        relu = place("relu", [P, 2, COLS], F32, at_tmp)
        square = place("square", [P, 2, COLS], F32, at_tmp, skip=2 * COLS)
        gated = place("gated", [P, TT, COLS], F32, at_tmp)
        four = place("four", [P, 2, N], F32, at_tmp)
        odd = place("odd", [P, 2, HALF], F32, at_tmp, skip=2 * N)
        rows = place("rows", [P, COLS], F32, at_tmp, skip=2 * N + 2 * HALF)
        hmod = place("hmod", [P, 2, N], F32, at_tmp)

        def small(name, shape):
            words = int(np.prod(shape[1:]))
            return place(name, shape, F32, region(words))

        ident = small("ident", [P, P])
        ones = small("ones", [P, P])
        vecs = small("vecs", [P, P])
        vec_t = small("vec_t", [P, P])
        c_rows = small("c_rows", [DT, P])
        c_exp = small("c_exp", [P, DT])
        c_den = small("c_den", [P, DT])
        c_t = small("c_t", [P, DT])
        silu = small("silu", [P, DT])
        at_silu32 = region(DT * 32)
        silu32 = place("silu32", [P, DT, 32], F32, at_silu32)
        block_junk = place("block_junk", [P, COLS], F32, at_silu32)
        shift32 = place("shift32", [P, DT, 32], F32, at_silu32)
        zero_freq = small("zero_freq", [P, DT])
        ssq_part = small("ssq_part", [P, TT, DB])
        mods = small("mods", [P, 6, DT])
        ssq = small("ssq", [P, 3, TT])
        rms = small("rms", [P, 3, TT])
        mean = small("mean", [P, 3, TT])
        inv = small("inv", [P, 3, TT])
        brow = gate[0:1, :]

        banks = ctx.enter_context(nc.psum_tensor("banks", [P, 8, COLS], F32))

        def sem(name):
            return ctx.enter_context(nc.semaphore(name))

        const_in = sem("const_in")
        brow_in = sem("brow_in")
        x_in = [sem(f"x_in{t}") for t in range(TT)]
        raw_full = [sem(f"raw_full{s}") for s in range(RAW)]
        ones_set = sem("ones_set")
        turned = sem("turned")
        vec_ready = sem("vec_ready")
        exp_done = sem("exp_done")
        silu_step = sem("silu_step")
        silu_ready = sem("silu_ready")
        sq_done = sem("sq_done")
        mean_done = sem("mean_done")
        rms_done = sem("rms_done")
        inv_done = sem("inv_done")
        xhi_done, xlo_done = sem("xhi_done"), sem("xlo_done")
        table_ready = sem("table_ready")
        spec_sum, spec_done = sem("spec_sum"), sem("spec_done")
        gemv_step = sem("gemv_step")
        col_sum = sem("col_sum")
        gemv_pe = sem("gemv_pe")
        rows_out, rows_turned = sem("rows_out"), sem("rows_turned")
        scale_sum = sem("scale_sum")
        shift_ready, shift_sum = sem("shift_ready"), sem("shift_sum")
        block0_out = sem("block0_out")
        zero_step = sem("zero_step")
        ssq_sum = sem("ssq_sum")
        gain_done = sem("gain_done")
        table_hi = sem("table_hi")
        mod_step = sem("mod_step")
        modp_hi, modp_lo = sem("modp_hi"), sem("modp_lo")
        chan_sum = sem("chan_sum")
        odd_zero, odd_done = sem("odd_zero"), sem("odd_done")
        four_done, four_hi, four_lo = sem("four_done"), sem("four_hi"), sem("four_lo")
        mirrored = sem("mirrored")
        gate_ready = sem("gate_ready")
        w_hi, w_lo, w_used = sem("w_hi"), sem("w_lo"), sem("w_used")
        y_read = sem("y_read")
        x_updated = sem("x_updated")
        tile_sum = sem("tile_sum")
        tile_gated = sem("tile_gated")
        tile_updated = sem("tile_updated")
        diag_ready = sem("diag_ready")
        h2_turned = sem("h2_turned")
        hmod_done, h2_hi, h2_lo = sem("hmod_done"), sem("h2_hi"), sem("h2_lo")
        h_relu, h_square, h_hi, h_lo = sem("h_relu"), sem("h_square"), sem("h_hi"), sem("h_lo")
        gfin_in = sem("gfin_in")
        y_normed, y_scaled = sem("y_normed"), sem("y_scaled")
        stored = sem("stored")

        HALVES = 2 * HB
        Y1 = DB

        block = ctx.enter_context(nc.Block())

        @block.sync
        def _(sp):
            def unit_source(w, chunk):
                if w[0] == "seq":
                    return seq_table.rearrange("(t p) n -> p t n", p=P)
                if w[0] == "cos":
                    return cos_table.rearrange("(t p) n -> p t n", p=P)
                if w[0] == "sin":
                    return sin_table.rearrange("(t p) n -> p t n", p=P)
                if w[0] == "ada":
                    return ada_v[:, w[2], w[1] * D:(w[1] + 1) * D]
                if w[0] == "mix":
                    return mix_v[:, UK * w[2]:UK * (w[2] + 1), COLS * w[1]:COLS * (w[1] + 1)]
                if w[0] == "up":
                    return up_v[:, UK * w[2]:UK * (w[2] + 1),
                                bass.ds(chunk * CH + COLS * w[1], COLS)]
                return down_v[:, bass.ds(chunk * HT + UK * w[2], UK), COLS * w[1]:COLS * (w[1] + 1)]

            def consumed(w):
                if w in pe_order:
                    return gemv_pe, pe_order.index(w) + 1
                if w[0] == "ada":
                    return gemv_step, ada_order.index(w) + 1
                if w in table_order:
                    return table_ready, table_order.index(w) + 1
                return w_lo, weight_order.index(w) + 1

            def load(w, slot, chunk=0):
                src = unit_source(w, chunk)
                dst = raw[:, slot, :]
                if len(src.shape) == 3:
                    dst = dst[:, 0:src.shape[1] * src.shape[2]].rearrange("p (a n) -> p a n", a=src.shape[1])
                sp.dma_start(dst, src).then_inc(raw_full[slot], 16)

            sp.dma_start(c_rows[:, :], c).then_inc(const_in, 16)
            sp.dma_start(vecs[:, :], vectors).then_inc(const_in, 16)
            for t in range(TT):
                sp.dma_start(xres[:, t, :], x[t * P:(t + 1) * P, :]).then_inc(x_in[t], 16)
            for u, w in enumerate(units):
                if u >= RAW:
                    sp.wait_ge(*consumed(units[u - RAW]))
                load(w, u % RAW)
            with sp.Fori(1, CHUNKS) as chunk:
                for j, w in enumerate(chunk_units):
                    sp.wait_ge(w_lo, chunk * CU + (MU + j - RAW + 1))
                    load(w, slot_of(chunk, j), chunk)
            for t in range(TT):
                sp.wait_ge(y_scaled, t + 1)
                sp.wait_ge(y_normed, t + 1)
                sp.dma_start(out[t * P:(t + 1) * P, :], xres[:, t, :]).then_inc(stored, 16)
            sp.wait_ge(stored, 16 * TT)

        @block.gpsimd
        def _(pool):
            pool.wait_ge(chan_sum, GROUPS * 2)
            pool.dma_start(brow, bias_rows[0:1, :]).then_inc(brow_in, 16)
            pool.wait_ge(x_updated, DB)
            pool.dma_start(brow, bias_rows[1:2, :]).then_inc(brow_in, 16)
            pool.wait_ge(col_sum, 4)
            pool.dma_start(gfin[:, :], g_final.to_broadcast([P, D])).then_inc(gfin_in, 16)
            pool.wait_ge(gfin_in, 16)
            for d in range(DB - 1):
                cols = slice(COLS * d, COLS * (d + 1))
                pool.wait_ge(x_updated, Y1 + DB * (CHUNKS - 1) + d + 1)
                nc.gpsimd.tensor_tensor(gained[:, :, cols], xres[:, :, cols],
                                        gfin[:, cols].unsqueeze(1).to_broadcast([P, TT, COLS]),
                                        ALU.mult).then_inc(gain_done, 1)
            cols = slice(COLS * (DB - 1), D)
            for t in range(TT):
                if t < TT - 1:
                    pool.wait_ge(tile_updated, TT + t)
                else:
                    pool.wait_ge(x_updated, Y1 + DB * CHUNKS)
                nc.gpsimd.tensor_tensor(gained[:, t, cols], xres[:, t, cols], gfin[:, cols], ALU.mult)\
                    .then_inc(gain_done, 1)

        @block.scalar
        def _(act):
            act.dma_start(ident[:, :], identity).then_inc(const_in, 16)
            act.wait_ge(vec_ready, 1)
            nc.scalar.activation(c_exp[:, :], c_t[:, :], ACT.Exp, scale=-1.0).then_inc(exp_done, 1)

            def root(stage):
                act.wait_ge(mean_done, stage + 1)
                nc.scalar.activation(rms[:, stage, :], mean[:, stage, :], ACT.Sqrt).then_inc(rms_done, 1)

            for t in range(TT):
                act.wait_ge(x_in[t], 16)
                if t >= 1:
                    act.wait_ge(sq_done, t)
                nc.scalar.activation(junk[:, :], xres[:, t, :], ACT.Square,
                                     accum_out=ssq[:, 0, t:t + 1]).then_inc(sq_done, 1)
            root(0)
            act.wait_ge(inv_done, 1)
            def table_high(dst, w):
                u = position[w]
                act.wait_ge(raw_full[u % RAW], filled[u])
                words = dst.shape[1] * dst.shape[2]
                nc.scalar.activation(dst, raw[:, u % RAW, 0:words].rearrange("p (a n) -> p a n", a=dst.shape[1]),
                                     ACT.Copy).then_inc(table_hi, 1)

            def evacuate_spec(d):
                act.wait_ge(spec_sum, d + 1)
                nc.scalar.activation(spec[:, d, :], banks[:, d % 4, :], ACT.Copy).then_inc(spec_done, 1)
                if d == LAST_SCALE:
                    rows_of(0)

            def rows_of(i):
                if i == 0:
                    act.wait_ge(scale_sum, 1)
                elif i == 1:
                    act.wait_ge(gemv_pe, len(pe_order))
                else:
                    act.wait_ge(shift_sum, 1)
                if i >= 1:
                    act.wait_ge(rows_turned, i)
                width = COLS if i < 2 else FT * P
                nc.scalar.activation(rows[:, 0:width], banks[:, (4, 5, 5)[i], 0:width], ACT.Copy)\
                    .then_inc(rows_out, 1)

            def spec_high(g):
                act.wait_ge(mod_step, 3)
                if g >= 2:
                    act.wait_ge(chan_sum, 2 * (g - 1))
                for d in range(GT * g, GT * (g + 1)):
                    nc.scalar.activation(modp[:, (g + 1) % 2, 0, d % GT, :], spec[:, d, :], ACT.Copy,
                                         scale=mods[:, SCALE1, d:d + 1]).then_inc(modp_hi, 1)

            for q in range(GROUPS):
                if q >= 2:
                    act.wait_ge(spec_sum, GT * (q - 1))
                for t in range(TT):
                    nc.scalar.activation(xsp[:, q % 2, 0, t, :], xres[:, t, q * GD:(q + 1) * GD], ACT.Copy,
                                         scale=inv[:, 0, t:t + 1]).then_inc(xhi_done, 1)
                if q == 0:
                    table_high(seqt[:, 0, :, :], ("seq",))
                if q >= 1:
                    for d in range(GT * (q - 1), GT * q):
                        evacuate_spec(d)
            for d in range(GT * (GROUPS - 1), DT):
                evacuate_spec(d)
                if d == DT - 3:
                    table_high(cost[:, 0, :, :], ("cos",))
                if d == DT - 2:
                    table_high(sint[:, 0, :, :], ("sin",))
                    spec_high(0)
            spec_high(1)
            for g in range(GROUPS):
                for h in range(2):
                    s = 2 * g + h
                    act.wait_ge(chan_sum, s + 1)
                    if s == 0:
                        act.wait_ge(odd_zero, 1)
                    if s >= 2:
                        act.wait_ge(four_done, FT * (g - 1) + (1 if h == 0 else FT))
                    nc.scalar.activation(odd[:, h, 1:HALF], banks[:, 2 * h + 1, 1:HALF], ACT.Copy)\
                        .then_inc(odd_done, 1)
                    for r in range(0, 1) if h == 0 else range(1, FT):
                        i = FT * g + r
                        act.wait_ge(four_done, i + 1)
                        nc.scalar.activation(fo[:, GT * g + (0, 1, 3)[r], 0, :], four[:, i % 2, :], ACT.Copy)\
                            .then_inc(four_hi, 1)
                act.wait_ge(four_lo, FT * g + 1)
                first, mirror = fo[:, GT * g, :, :], fo[:, GT * g + 2, :, :]
                nc.scalar.activation(mirror[:, :, 1:N], first[:, :, N - 1:0:-1].bitcast(F32), ACT.Copy)\
                    .then_inc(mirrored, 1)
                nc.scalar.activation(mirror[:, :, 0:1], first[:, :, 0:1].bitcast(F32), ACT.Copy)\
                    .then_inc(mirrored, 1)
                if g + 2 < GROUPS:
                    spec_high(g + 2)
            rows_of(1)

            def weight_high(slot, full, ws, used):
                act.wait_ge(raw_full[slot], full)
                if used is not None:
                    act.wait_ge(w_used, used)
                nc.scalar.activation(wsp[:, ws, 0, :, :], raw[:, slot, :].rearrange("p (a n) -> p a n", a=UK),
                                     ACT.Copy).then_inc(w_hi, 1)

            def block_squares(stage, d, y, tiles=range(TT)):
                if d < DB - 1:
                    act.wait_ge(x_updated, y)
                for t in tiles:
                    if d == DB - 1 and t < TT - 1:
                        act.wait_ge(tile_updated, (TT - 1) * (stage - 1) + t + 1)
                    elif d == DB - 1:
                        act.wait_ge(x_updated, y)
                    if stage_squares[0] > TT:
                        act.wait_ge(sq_done, stage_squares[0])
                    nc.scalar.activation(block_junk[:, :], xres[:, t, COLS * d:COLS * (d + 1)], ACT.Square,
                                         accum_out=ssq_part[:, t, d:d + 1]).then_inc(sq_done, 1)
                    stage_squares[0] += 1

            stage_squares = [TT]

            for n, w in enumerate(mix_units):
                u = position[("mix",) + w]
                if n == 1:
                    rows_of(2)
                if n == 0:
                    act.wait_ge(spec_sum, DT)
                weight_high(u % RAW, filled[u], (n + 1) % WS, n - WS + 1 if n >= WS else None)
                if n == 5:
                    act.wait_ge(w_used, DT // UK)
                    nc.scalar.activation(gated[:, :, :], banks[:, 0:4, :], ACT.Copy).then_inc(block0_out, 1)
                if n == GATE1_AT + 1:
                    act.wait_ge(col_sum, 1)
                    nc.scalar.activation(gate[:, :].rearrange("p (a n) -> p a n", a=DB),
                                         banks[:, 0:4, :], ACT.Copy).then_inc(gate_ready, 1)
                for d in range(DB - 1):
                    if n == UPDATED[d] + 1:
                        block_squares(1, d, d + 1)
            def chunk_high(chunk, j):
                weight_high(slot_of(chunk, j), full_at(chunk, j), (j + 1) % WS, MU + CU * chunk + j - WS + 1)

            chunk_high(0, 0)
            block_squares(1, DB - 1, DB)
            root(1)
            act.wait_ge(mod_step, MODS_READY)
            for k in range(DT):
                if k % UK == UK - 1 and k < DT - 1:
                    chunk_high(0, k // UK + 1)
                act.wait_ge(h2_turned, k + 1)
                if k >= 2:
                    act.wait_ge(h2_lo, k - 1)
                nc.scalar.activation(hmod[:, k % 2, :], banks[:, 4 + k % 4, :], ACT.Identity,
                                     scale=mods[:, SCALE2, k:k + 1],
                                     bias=mods[:, SHIFT2, k:k + 1]).then_inc(hmod_done, 1)
                act.wait_ge(hmod_done, k + 1)
                nc.scalar.activation(acts[:, k, 0, :], hmod[:, k % 2, :], ACT.Copy).then_inc(h2_hi, 1)

            def hidden_relu(chunk, g, half):
                h = HALVES * chunk + 2 * g + half
                act.wait_ge(w_used, CU * chunk + (MU + UP_END[g]))
                if half == 0 and g == 0:
                    act.wait_ge(x_updated, Y1 + DB * chunk)
                if half == 0:
                    act.wait_ge(h2_lo, DT)
                if not isinstance(h, int) or h >= 1:
                    act.wait_ge(h_square, h)
                b = 4 * (g % 2) + 2 * half
                nc.scalar.activation(relu[:, :, :], banks[:, b:b + 2, :], ACT.Relu).then_inc(h_relu, 1)

            def hidden_high(chunk, g, half):
                h = HALVES * chunk + 2 * g + half
                act.wait_ge(h_square, h + 1)
                t = 4 * g + 2 * half
                nc.scalar.activation(hid[:, t:t + 2, 0, :], square[:, :, :], ACT.Copy).then_inc(h_hi, 1)

            def chunk_body(chunk):
                for j in range(CU):
                    if not (isinstance(chunk, int) and chunk == 0 and j < DT // UK):
                        if j == DT // UK + 1 or j == 2 * (DT // UK) + 1:
                            if j == 2 * (DT // UK) + 1 and isinstance(chunk, int) and chunk == 0:
                                act.wait_ge(col_sum, 4)
                                nc.scalar.activation(gate[:, :].rearrange("p (a n) -> p a n", a=DB),
                                                     banks[:, 0:4, :], ACT.Copy).then_inc(gate_ready, 1)
                            hidden_relu(chunk, j // (DT // UK) - 1, 0)
                        chunk_high(chunk, j)
                        if j == DT // UK + 1 or j == 2 * (DT // UK) + 1:
                            g = j // (DT // UK) - 1
                            hidden_relu(chunk, g, 1)
                            hidden_high(chunk, g, 0)
                            hidden_high(chunk, g, 1)

            chunk_body(0)
            with act.Fori(1, CHUNKS) as chunk:
                chunk_body(chunk)
            for d in range(DB - 1):
                block_squares(2, d, Y1 + DB * (CHUNKS - 1) + d + 1)

            def scale_tile(t):
                act.wait_ge(inv_done, 3 + t)
                act.wait_ge(gain_done, DB + t)
                nc.scalar.activation(xres[:, t, 0:D // 2], gained[:, t, 0:D // 2], ACT.Copy,
                                     scale=inv[:, 2, t:t + 1]).then_inc(y_scaled, 1)

            for t in range(TT):
                block_squares(2, DB - 1, Y1 + DB * CHUNKS, [t])
                act.wait_ge(mean_done, 3 + t)
                nc.scalar.activation(rms[:, 2, t:t + 1], mean[:, 2, t:t + 1], ACT.Sqrt).then_inc(rms_done, 1)
                scale_tile(t)

        @block.vector
        def _(dve):
            nc.vector.memset(ones[:, :], 1.0).then_inc(ones_set, 1)
            dve.wait_ge(turned, 1)
            nc.vector.tensor_copy(c_t[:, :], banks[:, 1, 0:DT]).then_inc(vec_ready, 1)
            nc.vector.tensor_copy(vec_t[:, :], banks[:, 0, 0:P]).then_inc(vec_ready, 1)
            dve.wait_ge(exp_done, 1)
            nc.vector.tensor_scalar(c_den[:, :], c_exp[:, :], 1.0, None, ALU.add).then_inc(silu_step, 1)
            dve.wait_ge(silu_step, 1)
            nc.vector.reciprocal(c_exp[:, :], c_den[:, :]).then_inc(silu_step, 1)
            dve.wait_ge(silu_step, 2)
            nc.vector.tensor_tensor(silu[:, :], c_t[:, :], c_exp[:, :], ALU.mult).then_inc(silu_step, 1)
            dve.wait_ge(silu_step, 3)
            nc.vector.tensor_copy(silu32[:, :, :], silu[:, :].unsqueeze(2).to_broadcast([P, DT, 32]))\
                .then_inc(silu_ready, 1)

            def inverse(stage):
                dve.wait_ge(sq_done, TT + DB * TT * stage)
                if stage >= 1:
                    nc.vector.tensor_reduce(ssq[:, stage, :], ssq_part[:, :, :], mybir.AxisListType.X, ALU.add)\
                        .then_inc(ssq_sum, 1)
                    dve.wait_ge(ssq_sum, stage)
                nc.vector.tensor_scalar(mean[:, stage, :], ssq[:, stage, :], 1.0 / D, EPS,
                                        ALU.mult, ALU.add).then_inc(mean_done, 1)
                dve.wait_ge(rms_done, stage + 1)
                nc.vector.reciprocal(inv[:, stage, :], rms[:, stage, :]).then_inc(inv_done, 1)
                dve.wait_ge(inv_done, stage + 1)

            steps = [0]

            def gemv(j, k):
                u = position[("ada", j, k)]
                s = u % RAW
                acc = {SCALE1: acc_s, SHIFT2: acc_b}.get(j, acc_a)
                if k == 0:
                    if j == SHIFT2:
                        dve.wait_ge(chan_sum, 2 * GROUPS)
                    elif j in (SCALE2, GATE2):
                        dve.wait_ge(col_sum, {SCALE2: 1, GATE2: 3}[j])
                dve.wait_ge(raw_full[s], filled[u])
                if k == 0:
                    ins = nc.vector.tensor_scalar(acc[:, :], raw[:, s, :], silu[:, 0:1], None, ALU.mult)
                else:
                    dve.wait_ge(gemv_step, steps[0])
                    ins = nc.vector.scalar_tensor_tensor(acc[:, :], raw[:, s, :], silu[:, k:k + 1], acc[:, :],
                                                         ALU.mult, ALU.add)
                ins.then_inc(gemv_step, 1)
                steps[0] += 1

            def table_low(dst, hi, w, n):
                u = position[w]
                dve.wait_ge(table_hi, n)
                words = dst.shape[1] * dst.shape[2]
                nc.vector.tensor_tensor(dst, raw[:, u % RAW, 0:words].rearrange("p (a n) -> p a n", a=dst.shape[1]),
                                        hi.bitcast(F32), ALU.subtract).then_inc(table_ready, 1)

            def x_low(q):
                for t in range(TT):
                    dve.wait_ge(xhi_done, TT * q + t + 1)
                    nc.vector.scalar_tensor_tensor(
                        xsp[:, q % 2, 1, t, :], xres[:, t, q * GD:(q + 1) * GD], inv[:, 0, t:t + 1],
                        xsp[:, q % 2, 0, t, :].bitcast(F32), ALU.mult, ALU.subtract).then_inc(xlo_done, 1)

            inverse(0)
            x_low(0)
            table_low(seqt[:, 1, :, :], seqt[:, 0, :, :], ("seq",), 1)
            scale_left = [k for k in range(DT) if k % SHARE != SHARE - 1]
            for q, count in zip(range(1, GROUPS + 1), (1, 4, 3, len(scale_left))):
                for _ in range(min(count, len(scale_left))):
                    gemv(SCALE1, scale_left.pop(0))
                if q < GROUPS:
                    x_low(q)

            def add_bias(j, sums):
                nc.vector.tensor_tensor(mods[:, j, :], sums, vec_t[:, j * DT:(j + 1) * DT], ALU.add)\
                    .then_inc(mod_step, 1)

            def times_gain(j, gain):
                nc.vector.scalar_tensor_tensor(mods[:, j, :], mods[:, j, :], 1.0, gain, ALU.add,
                                               ALU.mult).then_inc(mod_step, 1)

            def turned_rows(j, bank):
                dve.wait_ge(vec_ready, 2)
                sums = banks[:, bank, :].rearrange("p (b a r) -> p a b r", b=4, a=4)[:, :, :, 0]
                nc.vector.tensor_tensor(mods[:, j, :].rearrange("p (a b) -> p a b", a=4), sums,
                                        vec_t[:, j * DT:(j + 1) * DT].rearrange("p (a b) -> p a b", a=4),
                                        ALU.add).then_inc(mod_step, 1)

            dve.wait_ge(rows_turned, 1)
            turned_rows(SCALE1, 6)
            dve.wait_ge(mod_step, 1)
            times_gain(SCALE1, vec_t[:, 6 * DT:7 * DT])
            dve.wait_ge(mod_step, 2)
            nc.vector.tensor_scalar(mods[:, SCALE1, :], mods[:, SCALE1, :], NORM, None, ALU.mult)\
                .then_inc(mod_step, 1)
            dve.wait_ge(mod_step, 3)
            nc.vector.memset(odd[:, :, 0:1], 0.0).then_inc(odd_zero, 1)

            def spec_low(g):
                for d in range(GT * g, GT * (g + 1)):
                    dve.wait_ge(modp_hi, d + 1)
                    nc.vector.scalar_tensor_tensor(
                        modp[:, (g + 1) % 2, 1, d % GT, :], spec[:, d, :], mods[:, SCALE1, d:d + 1],
                        modp[:, (g + 1) % 2, 0, d % GT, :].bitcast(F32), ALU.mult, ALU.subtract).then_inc(modp_lo, 1)

            def four_tile(i):
                g, kind = i // FT, i % FT
                tile = GT * g + (0, 1, 3)[kind]
                h = 0 if kind == 0 else 1
                dve.wait_ge(odd_done, 2 * g + h + 1)
                even = banks[:, (0, 2, 6)[kind], :]
                if i >= 2:
                    dve.wait_ge(four_lo, i - 1)
                    dve.wait_ge(four_hi, i - 1)
                near, far = (ALU.subtract, ALU.add) if kind < 2 else (ALU.add, ALU.subtract)
                nc.vector.tensor_tensor(four[:, i % 2, 0:HALF], even[:, 0:HALF], odd[:, h, :], near)
                nc.vector.tensor_tensor(four[:, i % 2, N - 1:HALF:-1], even[:, 1:HALF], odd[:, h, 1:HALF], far)
                nc.vector.tensor_copy(four[:, i % 2, HALF:HALF + 1], even[:, HALF:HALF + 1])\
                    .then_inc(four_done, 1)
                dve.wait_ge(four_hi, i + 1)
                nc.vector.tensor_tensor(fo[:, tile, 1, :], four[:, i % 2, :], fo[:, tile, 0, :].bitcast(F32),
                                        ALU.subtract).then_inc(four_lo, 1)

            table_low(cost[:, 1, :, :], cost[:, 0, :, :], ("cos",), 2)
            table_low(sint[:, 1, :, :], sint[:, 0, :, :], ("sin",), 3)
            spec_low(0)
            spec_low(1)
            for i in range(GROUPS * FT):
                four_tile(i)
                if i % FT == FT - 1 and i // FT + 2 < GROUPS:
                    spec_low(i // FT + 2)
            dve.wait_ge(rows_turned, 2)
            turned_rows(SHIFT1, 7)
            dve.wait_ge(mod_step, 4)
            nc.vector.tensor_scalar(mods[:, SHIFT1, :], mods[:, SHIFT1, :], N * NORM, None, ALU.mult)\
                .then_inc(mod_step, 1)
            dve.wait_ge(mod_step, MODS1)
            nc.vector.tensor_copy(shift32[:, :, :], mods[:, SHIFT1, :].unsqueeze(2).to_broadcast([P, DT, 32]))\
                .then_inc(shift_ready, 1)

            def shift_token():
                dve.wait_ge(mirrored, 2 * GROUPS)
                nc.vector.tensor_tensor(zero_freq[:, :], fo[:, :, 0, 0].bitcast(F32), fo[:, :, 1, 0].bitcast(F32),
                                        ALU.add).then_inc(zero_step, 1)
                dve.wait_ge(rows_turned, 3)
                dve.wait_ge(zero_step, 1)
                sums = banks[:, 7, 0:FT * P].rearrange("p (b g r) -> p g b r", b=FT, g=GROUPS)[:, :, :, 0]
                tiles = zero_freq[:, :].rearrange("p (g i) -> p g i", g=GROUPS)
                nc.vector.tensor_tensor(tiles[:, :, 0:2], tiles[:, :, 0:2], sums[:, :, 0:2], ALU.add)\
                    .then_inc(zero_step, 1)
                nc.vector.tensor_tensor(tiles[:, :, 2:4], tiles[:, :, 2:4], sums[:, :, 0:3:2], ALU.add)\
                    .then_inc(zero_step, 1)
                dve.wait_ge(zero_step, 3)
                nc.vector.tensor_copy(fo[:, :, 0, 0], zero_freq[:, :]).then_inc(zero_step, 1)
                dve.wait_ge(zero_step, 4)
                nc.vector.tensor_tensor(fo[:, :, 1, 0], zero_freq[:, :], fo[:, :, 0, 0].bitcast(F32),
                                        ALU.subtract).then_inc(zero_step, 1)

            def weight_low(slot, ws, n):
                dve.wait_ge(w_hi, n + 1)
                nc.vector.tensor_tensor(wsp[:, ws, 1, :, :],
                                        raw[:, slot, :].rearrange("p (a n) -> p a n", a=UK),
                                        wsp[:, ws, 0, :, :].bitcast(F32), ALU.subtract).then_inc(w_lo, 1)

            def update_x(y, b, d, gates, done, source=None):
                dve.wait_ge(w_used, done)
                dve.wait_ge(gate_ready, gates)
                if not isinstance(y, int) or y >= 1:
                    dve.wait_ge(x_updated, y)
                cols = slice(COLS * d, COLS * (d + 1))
                nc.vector.tensor_tensor(gated[:, :, :], banks[:, b:b + 4, :] if source is None else source,
                                        gate[:, cols].unsqueeze(1).to_broadcast([P, TT, COLS]),
                                        ALU.mult).then_inc(y_read, 1)
                dve.wait_ge(y_read, y + 1)
                nc.vector.tensor_tensor(xres[:, :, cols], xres[:, :, cols], gated[:, :, :],
                                        ALU.add).then_inc(x_updated, 1)

            def update_tiles(i, y, gates, done, after=None):
                d = DB - 1
                before = (TT - 1) * CHUNKS * i
                cols = slice(COLS * d, COLS * (d + 1))
                dve.wait_ge(gate_ready, gates)
                dve.wait_ge(x_updated, y)
                for t in range(TT):
                    last = t == TT - 1
                    if last:
                        dve.wait_ge(w_used, done)
                    else:
                        dve.wait_ge(tile_sum, before + t + 1)
                    nc.vector.tensor_tensor(gated[:, t, :], banks[:, 4 + t, :], gate[:, cols], ALU.mult)\
                        .then_inc(y_read if last else tile_gated, 1)
                    if last:
                        dve.wait_ge(y_read, y + 1)
                    else:
                        dve.wait_ge(tile_gated, (TT - 1) * i + t + 1)
                    nc.vector.tensor_tensor(xres[:, t, cols], xres[:, t, cols], gated[:, t, :], ALU.add)\
                        .then_inc(x_updated if last else tile_updated, 1)
                    if after is not None:
                        after(t)

            for n, w in enumerate(mix_units):
                u = position[("mix",) + w]
                weight_low(u % RAW, (n + 1) % WS, n)
                for i, (_, j, k) in enumerate(runs[n]):
                    gemv(j, k)
                    if n == 0 and i == 0:
                        shift_token()
                if n in UPDATED:
                    y = UPDATED.index(n)
                    if y == 0:
                        dve.wait_ge(block0_out, 1)
                    update_x(y, 4 * (y % 2), y, 1, (y + 1) * (DT // UK), gated[:, :, :] if y == 0 else None)
            weight_low(slot_of(0, 0), 1, MU)
            update_tiles(0, DB - 1, 1, MU)
            inverse(1)
            nc.vector.tensor_tensor(diag[:, :, :], ident[:, :].unsqueeze(1).to_broadcast([P, TT, P]),
                                    inv[:, 1, :].unsqueeze(2).to_broadcast([P, TT, P]), ALU.mult)\
                .then_inc(diag_ready, 1)
            dve.wait_ge(col_sum, 3)
            add_bias(SHIFT2, banks[:, 0, 0:DT])
            add_bias(SCALE2, banks[:, 0, DT:2 * DT])
            dve.wait_ge(mod_step, MODS_READY - 1)
            times_gain(SCALE2, vec_t[:, 7 * DT:8 * DT])

            def gate2(j):
                for k in range(per_up * j, per_up * (j + 1)):
                    gemv(GATE2, k)

            for k in range(DT):
                if k % UK == UK - 1 and k < DT - 1:
                    j = k // UK + 1
                    weight_low(slot_of(0, j), (j + 1) % WS, MU + j)
                    gate2(j - 1)
                dve.wait_ge(h2_hi, k + 1)
                nc.vector.tensor_tensor(acts[:, k, 1, :], hmod[:, k % 2, :], acts[:, k, 0, :].bitcast(F32),
                                        ALU.subtract).then_inc(h2_lo, 1)

            def hidden_square(chunk, g, half):
                h = HALVES * chunk + 2 * g + half
                dve.wait_ge(h_relu, h + 1)
                if not isinstance(h, int) or h >= 1:
                    dve.wait_ge(h_lo, h)
                nc.vector.tensor_tensor(square[:, :, :], relu[:, :, :], relu[:, :, :], ALU.mult)\
                    .then_inc(h_square, 1)

            def hidden_low(chunk, g, half):
                h = HALVES * chunk + 2 * g + half
                dve.wait_ge(h_hi, h + 1)
                t = 4 * g + 2 * half
                nc.vector.tensor_tensor(hid[:, t:t + 2, 1, :], square[:, :, :], hid[:, t:t + 2, 0, :].bitcast(F32),
                                        ALU.subtract).then_inc(h_lo, 1)

            def chunk_body(chunk):
                first = isinstance(chunk, int) and chunk == 0
                for j in range(CU):
                    hidden = j == DT // UK + 1 or j == 2 * (DT // UK) + 1
                    g = j // (DT // UK) - 1
                    if hidden:
                        hidden_square(chunk, g, 0)
                    if not (first and j < DT // UK):
                        weight_low(slot_of(chunk, j), (j + 1) % WS, MU + CU * chunk + j)
                    if hidden:
                        hidden_low(chunk, g, 0)
                        hidden_square(chunk, g, 1)
                        hidden_low(chunk, g, 1)
                    if first and DT // UK - 1 <= j < len(up_units):
                        gate2(j)
                    if j == 1 and not first:
                        update_x(DB * chunk + (Y1 - 1), 4, DB - 1, 2, CU * chunk + MU)
                    for d in range(DB - 1):
                        if j == DOWN_END[d] + 1:
                            update_x(DB * chunk + (Y1 + d), 4 * (d % 2), d, 2, CU * chunk + (MU + DOWN_END[d]))

            chunk_body(0)
            with dve.Fori(1, CHUNKS) as chunk:
                chunk_body(chunk)

            def scale_half(t):
                dve.wait_ge(inv_done, 3 + t)
                dve.wait_ge(gain_done, DB + t)
                nc.vector.tensor_scalar(xres[:, t, D // 2:], gained[:, t, D // 2:], inv[:, 2, t:t + 1], None,
                                        ALU.mult).then_inc(y_normed, 1)

            def invert_tile(t):
                if t >= 1:
                    scale_half(t - 1)
                dve.wait_ge(sq_done, TT + DB * TT + (DB - 1) * TT + t + 1)
                nc.vector.tensor_reduce(ssq[:, 2, t:t + 1], ssq_part[:, t, :], mybir.AxisListType.X, ALU.add)\
                    .then_inc(ssq_sum, 1)
                dve.wait_ge(ssq_sum, 2 + t)
                nc.vector.tensor_scalar(mean[:, 2, t:t + 1], ssq[:, 2, t:t + 1], 1.0 / D, EPS,
                                        ALU.mult, ALU.add).then_inc(mean_done, 1)
                dve.wait_ge(rms_done, 3 + t)
                nc.vector.reciprocal(inv[:, 2, t:t + 1], rms[:, 2, t:t + 1]).then_inc(inv_done, 1)

            update_tiles(1, Y1 + DB * CHUNKS - 1, 2, MU + CU * CHUNKS, invert_tile)
            scale_half(TT - 1)

        @block.tensor
        def _(pe):
            def product(bank, w_hi_ap, w_lo_ap, m_hi, m_lo, first, last):
                nc.tensor.matmul(bank, w_hi_ap, m_hi, start=first, stop=False)
                nc.tensor.matmul(bank, w_hi_ap, m_lo, start=False, stop=False)
                return nc.tensor.matmul(bank, w_lo_ap, m_hi, start=False, stop=last)

            pe.wait_ge(const_in, 48)
            nc.tensor.transpose(banks[:, 0, 0:P], vecs[:, :], ident[:, :])
            nc.tensor.transpose(banks[:, 1, 0:DT], c_rows[:, :], ident[0:DT, 0:DT]).then_inc(turned, 1)
            pe.wait_ge(vec_ready, 2)
            def gemv_rows(i, k):
                u = position[("ada", (SCALE1, SHIFT1)[i], k)]
                pe.wait_ge(raw_full[u % RAW], filled[u])
                for a in range(4):
                    mm = nc.tensor.matmul(banks[32 * a:32 * (a + 1), 4 + i, :], silu32[:, k, :],
                                          raw[:, u % RAW, COLS * a:COLS * (a + 1)], start=(k == (SHARE - 1, 0)[i]),
                                          stop=(i == 1 and k == DT - 1))
                mm.then_inc(gemv_pe, 1)

            def turn_rows(i, bank, blocks=4):
                pe.wait_ge(rows_out, i + 1)
                for b in range(blocks):
                    mm = nc.tensor.transpose(banks[:, bank, P * b:P * (b + 1)], rows[:, P * b:P * (b + 1)],
                                             ident[:, :])
                mm.then_inc(rows_turned, 1)

            pe.wait_ge(silu_ready, 1)
            pe.wait_ge(table_ready, 1)
            for d in range(DT):
                q = d // GT
                pe.wait_ge(xlo_done, TT * (q + 1))
                if d >= 4:
                    pe.wait_ge(spec_done, d - 3)
                cols = slice(P * (d % GT), P * (d % GT + 1))
                for t in range(TT):
                    mm = product(banks[:, d % 4, :], xsp[:, q % 2, 0, t, cols], xsp[:, q % 2, 1, t, cols],
                                 seqt[:, 0, t, :], seqt[:, 1, t, :], t == 0, t == TT - 1)
                mm.then_inc(spec_sum, 1)
                if d % SHARE == 0:
                    gemv_rows(0, d + SHARE - 1)
                if d == LAST_SCALE:
                    pe.wait_ge(ones_set, 1)
                    pe.wait_ge(gemv_step, SCALE1_STEPS)
                    for a in range(4):
                        mm = nc.tensor.matmul(banks[32 * a:32 * (a + 1), 4, :], ones[:, 0:32],
                                              acc_s[:, COLS * a:COLS * (a + 1)], start=False, stop=True)
                    mm.then_inc(scale_sum, 1)
                if d == LAST_SCALE + 1:
                    turn_rows(0, 6)

            def column_sums(acc, bank, col):
                for d in range(DT):
                    mm = nc.tensor.matmul(banks[:, bank, col + d:col + d + 1], acc[:, P * d:P * (d + 1)],
                                          ones[:, 0:1], start=(d == 0 and col == 0), stop=True, skip_group_check=True)
                mm.then_inc(col_sum, 1)

            def row_sums(acc, bank, rows):
                pe.wait_ge(brow_in, 16 * rows)
                for d in range(DB):
                    cols = slice(COLS * d, COLS * (d + 1))
                    nc.tensor.matmul(banks[:, bank + d, :], ones[0:1, :], brow[0:1, cols], start=True, stop=False)
                    mm = nc.tensor.matmul(banks[:, bank + d, :], ones[:, :], acc[:, cols], start=False, stop=True)
                mm.then_inc(col_sum, 1)

            shift_tiles = list(range(DT))
            pe.wait_ge(table_ready, 3)
            pe.wait_ge(spec_done, DT)
            for g in range(GROUPS):
                pe.wait_ge(modp_lo, GT * (g + 1))
                for h in range(2):
                    if g >= 1:
                        pe.wait_ge(four_done, FT * (g - 1) + (1 if h == 0 else FT))
                    if g == 0 and h == 1:
                        pe.wait_ge(mod_step, 1)
                    for kind, bank in ((0, 0),) if h == 0 else ((1, 2), (2, 6)):
                        cols = slice(P * kind, P * (kind + 1))
                        for d in range(GT):
                            product(banks[:, bank, 0:HALF + 2], cost[:, 0, d, cols], cost[:, 1, d, cols],
                                    modp[:, (g + 1) % 2, 0, d, 0:HALF + 2], modp[:, (g + 1) % 2, 1, d, 0:HALF + 2],
                                    d == 0, d == GT - 1)
                    cols = slice(P * h, P * (h + 1))
                    for d in range(GT):
                        mm = product(banks[:, 2 * h + 1, 0:HALF], sint[:, 0, d, cols], sint[:, 1, d, cols],
                                     modp[:, (g + 1) % 2, 0, d, HALF:], modp[:, (g + 1) % 2, 1, d, HALF:],
                                     d == 0, d == GT - 1)
                    mm.then_inc(chan_sum, 1)
                    for _ in range(1 if g == 0 else 2):
                        gemv_rows(1, shift_tiles.pop(0))
            for k in shift_tiles:
                gemv_rows(1, k)
            turn_rows(1, 7)

            def transform_shift():
                pe.wait_ge(shift_ready, 1)
                for d in range(GT):
                    for part in range(2):
                        for g in range(GROUPS):
                            mm = nc.tensor.matmul(banks[32 * g:32 * (g + 1), 5, 0:FT * P],
                                                  shift32[:, GT * g + d, :], cost[:, part, d, :].bitcast(F32),
                                                  start=(d == 0 and part == 0), stop=(d == GT - 1 and part == 1))
                mm.then_inc(shift_sum, 1)

            def token_unit(b, ws, n, left, q, k_tiles, by_tile=False, tiles=range(TT), steps={}):
                pe.wait_ge(w_lo, n + 1)
                for i in range(TT):
                    t = tiles[i]
                    if i in steps:
                        steps[i]()
                    tok = slice(P * t, P * (t + 1))
                    for kk in range(UK):
                        k = UK * q + kk
                        mm = product(banks[:, b + t, :], left[:, k, 0, tok], left[:, k, 1, tok],
                                     wsp[:, ws, 0, kk, :], wsp[:, ws, 1, kk, :], k == 0, k == k_tiles - 1)
                    if by_tile and t < TT - 1:
                        mm.then_inc(tile_sum, 1)
                mm.then_inc(w_used, 1)

            shift_steps = {1: transform_shift, 2: lambda: turn_rows(2, 7, FT), 3: lambda: pe.wait_ge(zero_step, 5)}
            for n, (d, q) in enumerate(mix_units):
                if q == 0:
                    if d == 1:
                        pe.wait_ge(zero_step, 5)
                    elif d == 2:
                        pe.wait_ge(gate_ready, 1)
                    elif d == 3:
                        pe.wait_ge(y_read, 2)
                if n == GATE1_AT:
                    pe.wait_ge(block0_out, 1)
                    pe.wait_ge(gemv_step, SCALE1_STEPS + DT)
                    row_sums(acc_a, 0, 1)
                token_unit(4 * (d % 2), (n + 1) % WS, n, fo, q, DT, by_tile=n == MU - 1,
                           tiles=(1, 2, 3, 0) if n == 0 else range(TT), steps=shift_steps if n == 0 else {})
            pe.wait_ge(y_read, DB - 1)
            pe.wait_ge(gemv_step, SCALE1_STEPS + 2 * DT)
            column_sums(acc_b, 0, 0)
            pe.wait_ge(gemv_step, SCALE1_STEPS + 3 * DT)
            column_sums(acc_a, 0, DT)

            def turn_tokens(k):
                if k >= 4:
                    pe.wait_ge(hmod_done, k - 3)
                for t in range(TT):
                    mm = nc.tensor.matmul(banks[:, 4 + k % 4, P * t:P * (t + 1)],
                                          xres[:, t, P * k:P * (k + 1)], diag[:, t, :], start=(t == 0), stop=True,
                                          skip_group_check=True)
                mm.then_inc(h2_turned, 1)

            LEAD = 3
            pe.wait_ge(diag_ready, 1)
            for k in range(LEAD):
                turn_tokens(k)

            def chunk_body(chunk):
                first = isinstance(chunk, int) and chunk == 0
                for j, (what, a, q) in enumerate(chunk_units):
                    n = MU + CU * chunk + j
                    b = 4 * (a % 2)
                    if what == "up":
                        if q == 0:
                            pe.wait_ge(y_read, Y1 + DB * chunk - 1 + a)
                            if first and a == 0:
                                pe.wait_ge(mod_step, MODS_READY)
                        pe.wait_ge(w_lo, n + 1)
                        for kk in range(UK):
                            k = UK * q + kk
                            if first and a == 0:
                                if k + LEAD < DT:
                                    turn_tokens(k + LEAD)
                                pe.wait_ge(h2_lo, k + 1)
                            for f in range(4):
                                cols = slice(P * f, P * (f + 1))
                                mm = product(banks[:, b + f, :], wsp[:, (j + 1) % WS, 0, kk, cols],
                                             wsp[:, (j + 1) % WS, 1, kk, cols], acts[:, k, 0, :], acts[:, k, 1, :],
                                             k == 0, k == DT - 1)
                        mm.then_inc(w_used, 1)
                        if first and j == len(up_units) - 1:
                            pe.wait_ge(h_relu, 2)
                            pe.wait_ge(gemv_step, SCALE1_STEPS + 4 * DT)
                            row_sums(acc_a, 0, 2)
                            pe.wait_ge(gate_ready, 2)
                    else:
                        if q == 0:
                            if a < 2:
                                pe.wait_ge(h_relu, HALVES * chunk + 2 * (a + 1))
                            else:
                                pe.wait_ge(y_read, Y1 + DB * chunk + a - 1)
                        pe.wait_ge(h_lo, HALVES * chunk + 2 * (q + 1))
                        token_unit(b, (j + 1) % WS, n, hid, q, HT, by_tile=j == CU - 1)

            chunk_body(0)
            with pe.Fori(1, CHUNKS) as chunk:
                chunk_body(chunk)


INPUTS = ("x", "c", "w_ada", "vectors", "bias_rows", "g_final", "w_mix", "w_ffn_in", "w_ffn_out",
          "seq_table", "cos_table", "sin_table", "identity")


def fourier_tables(n):
    a = np.arange(n)
    angle = 2 * np.pi * (np.outer(a, a) % n) / n
    cos, sin = np.cos(angle), np.sin(angle)
    half = n // 2
    seq = np.concatenate([cos[:, :half + 1], sin[:, 1:half]], axis=1)
    kept = np.concatenate([cos[:, 1:half + 1], cos[:, half // 2 + 1:half], cos[:, :1]], axis=1)
    return [t.astype(np.float32) for t in (seq, kept, sin[:, 1:half + 1])]


def mirrored_rows(w, groups):
    size = w.shape[0] // groups
    half = size // 2
    order = np.r_[1:half + 1, size - 1:half:-1, 0]
    return w.reshape(groups, size, -1)[:, order].reshape(w.shape)


def kernel(**inputs):
    import concourse.bacc as bacc
    from concourse.bass_utils import run_bass_kernel_spmd

    a = {k: np.ascontiguousarray(np.asarray(v)) for k, v in inputs.items()}
    n, d = a["x"].shape[1:]
    b_ada = a["b_ada"][0]
    seq_table, cos_table, sin_table = fourier_tables(n)
    data = {
        "x": a["x"][0], "c": a["c"].reshape(d // 128, 128), "w_ada": a["w_ada"][0],
        "vectors": np.concatenate([b_ada, a["g_norm_mix"][0], a["g_norm_ffn"][0]]).reshape(-1, 128),
        "bias_rows": np.stack([b_ada[2 * d:3 * d], b_ada[5 * d:6 * d]]),
        "g_final": a["g_final"].reshape(1, d), "w_mix": mirrored_rows(a["fno_w_out"][0], 4),
        "w_ffn_in": a["w_ffn_in"][0], "w_ffn_out": a["w_ffn_out"][0],
        "seq_table": seq_table, "cos_table": cos_table, "sin_table": sin_table, "identity": np.eye(128, dtype=np.float32),
    }
    data = {f"in_{k}": np.ascontiguousarray(data[k]) for k in INPUTS}
    nc = bacc.Bacc("TRN2", target_bir_lowering=False, num_devices=1, dynamic_dma_scratch_size=1024)
    aps = [nc.dram_tensor(k, v.shape, mybir.dt.from_np(v.dtype), kind="ExternalInput").ap()
           for k, v in data.items()]
    out = nc.dram_tensor("out", (n, d), mybir.dt.float32, kind="ExternalOutput").ap()
    fourier_ffn_block(nc, *aps, out)
    result = run_bass_kernel_spmd(nc, [data], core_ids=[0])
    return result.results[0]["out"].reshape(1, n, d)
```

```python
import math
from contextlib import ExitStack

import numpy as np

import concourse.bass as bass
from concourse import mybir


def fourier_ffn_block(nc, x, c, w_ada, vectors, bias_rows, g_final, w_mix, w_ffn_in, w_ffn_out,
                      seq_table, cos_table, sin_table, identity, out):
    F32, F32R = mybir.dt.float32, mybir.dt.float32r
    ALU, ACT = mybir.AluOpType, mybir.ActivationFunctionType

    P = 128
    N, D = x.shape
    FF = w_ffn_in.shape[1]
    TT = N // P
    DT = D // P
    GROUPS = 4
    GD = D // GROUPS
    GT = GD // P
    FT = 3
    HALF = N // 2
    COLS = 512
    UK = 4
    UNIT = UK * COLS
    DB = D // COLS
    CH = 1024
    CHUNKS = FF // CH
    HT = CH // P
    RAW = 4
    WS = 2
    EPS = 1e-6
    NORM = 1.0 / math.sqrt(N * GD)
    assert N == GD == COLS and D == UNIT

    SHIFT_LAST = 4
    LATE = 5
    SHARE = 4
    SHIFT1, SCALE1, GATE1, SHIFT2, SCALE2, GATE2 = range(6)
    units = [("seq",)] + [("ada", SCALE1, k) for k in range(DT)]
    units += [("cos",), ("sin",)] + [("ada", SHIFT1, k) for k in range(DT)]
    mix_units = [(d, q) for d in range(DB) for q in range(GROUPS)]
    others = [("ada", j, k) for j in (GATE1, SHIFT2, SCALE2) for k in range(DT)]
    between = [3] + [2] + [3] * 11 + [2] + [3] + [LATE]
    assert sum(between) == len(others)
    runs = []
    for i, w in enumerate(mix_units):
        runs.append(others[:between[i]])
        others = others[between[i]:]
        units.insert(len(units) - SHIFT_LAST * (i == 0), ("mix",) + w)
        units += [("up", 0, 0)] * (i == len(mix_units) - 1) + runs[-1]
    HB = CH // COLS
    up_units = [("up", g, q) for g in range(HB) for q in range(DT // UK)]
    down_units = [("down", 0, 0), ("down", 1, 0), ("down", 0, 1), ("down", 1, 1),
                  ("down", 2, 0), ("down", 2, 1), ("down", 3, 0), ("down", 3, 1)]
    chunk_units = up_units + down_units
    UP_END = [1 + max(j for j, w in enumerate(chunk_units) if w[:2] == ("up", g)) for g in range(HB)]
    DOWN_END = [1 + max(j for j, w in enumerate(chunk_units) if w[:2] == ("down", d)) for d in range(DB)]
    LAST_SCALE = DT - SHARE
    MODS1 = 5
    MODS_READY = MODS1 + 3
    per_up = DT // len(up_units)
    for i, w in enumerate(up_units):
        units += [w] * (i > 0) + [("ada", GATE2, k) for k in range(per_up * i, per_up * (i + 1))]
    units += down_units
    LATER = len(units)
    CU = len(chunk_units)
    assert CU % RAW == 0 and CU % WS == 0 and len(mix_units) % WS == 0
    MU = len(mix_units)
    GATE1_AT = 6
    UPDATED = [7, 9, 13]
    pe_order = [("ada", SCALE1, k) for k in range(DT) if k % SHARE == SHARE - 1]
    pe_order += [("ada", SHIFT1, k) for k in range(DT)]
    pe_order += [("ada", SCALE2, k) for k in range(DT - LATE, DT)]
    ada_order = [w for w in units if w[0] == "ada" and w not in pe_order]
    SCALE1_STEPS = sum(w[1] == SCALE1 for w in ada_order)
    table_order = [("seq",), ("cos",), ("sin",)]
    weight_order = [w for w in units if w[0] in ("mix", "up", "down")]
    position = {("c0",) + w if w[0] in ("up", "down") else w: u for u, w in enumerate(units)}

    def unit_at(chunk, j):
        if isinstance(chunk, int) and chunk == 0:
            return position[("c0",) + chunk_units[j]]
        return (chunk - 1) * CU + (LATER + j)

    def slot_of(chunk, j):
        return unit_at(0, j) % RAW if isinstance(chunk, int) and chunk == 0 else (LATER + j) % RAW

    fills = [0] * RAW
    filled = []
    for u, w in enumerate(units):
        fills[u % RAW] += 16
        filled.append(fills[u % RAW])

    def full_at(chunk, j):
        if isinstance(chunk, int) and chunk == 0:
            return filled[unit_at(0, j)]
        return (chunk - 1) * (16 * CU // RAW) + (fills[(LATER + j) % RAW] + 16 * (j // RAW + 1))

    ada_v = w_ada.rearrange("(k p) n -> p k n", p=P)
    mix_v = w_mix.rearrange("(k p) n -> p k n", p=P)
    up_v = w_ffn_in.rearrange("(k p) n -> p k n", p=P)
    down_v = w_ffn_out.rearrange("(k p) n -> p k n", p=P)

    with ExitStack() as ctx:
        top = [nc.sbuf_base + (-nc.sbuf_base) % 32]

        def region(words):
            at = top[0]
            top[0] += (4 * words + 31) // 32 * 32
            assert top[0] <= nc.sbuf_usable_end
            return at

        def place(name, shape, dt, at, skip=0):
            return nc.alloc_sbuf_tensor_at(name, shape, dt, offset=at + 4 * skip)

        at_x, at_acts, at_hid, at_w = (region(TT * D), region(2 * DT * N), region(2 * HT * N),
                                       region(2 * WS * UNIT))
        at_raw, at_gate, at_acc, at_tmp = region(RAW * UNIT), region(D), region(D), region(D)
        xres = place("xres", [P, TT, D], F32, at_x)
        acts = place("acts", [P, DT, 2, N], F32R, at_acts)
        fo = place("fo", [P, DT, 2, N], F32R, at_acts)
        spec = place("spec", [P, DT, N], F32, at_acts, skip=DT * N)
        hid = place("hid", [P, HT, 2, N], F32R, at_hid)
        seqt = place("seqt", [P, 2, TT, N], F32R, at_hid)
        modp = place("modp", [P, 2, 2, GT, N], F32R, at_hid)
        acc_b = place("acc_b", [P, D], F32, at_hid, skip=2 * HT * N - D)
        diag = place("diag", [P, TT, P], F32, at_hid)
        rows_late = place("rows_late", [P, COLS], F32, at_hid, skip=TT * P)
        wsp = place("wsp", [P, WS, 2, UK, COLS], F32R, at_w)
        xsp = place("xsp", [P, 2, 2, TT, GD], F32R, at_w)
        cost = place("cost", [P, 2, GT, 3 * P], F32R, at_w)
        sint = place("sint", [P, 2, GT, 2 * P], F32R, at_gate)
        raw = place("raw", [P, RAW, UNIT], F32, at_raw)
        gate = place("gate", [P, D], F32, at_gate)
        acc_a = place("acc_a", [P, D], F32, at_acc)
        acc_s = place("acc_s", [P, D], F32, at_gate)
        gfin = place("gfin", [P, D], F32, at_acc)
        gained = place("gained", [P, TT, D], F32, at_acts)
        junk = place("junk", [P, D], F32, at_tmp)
        relu = place("relu", [P, 2, COLS], F32, at_tmp)
        square = place("square", [P, 2, COLS], F32, at_tmp, skip=2 * COLS)
        gated = place("gated", [P, TT, COLS], F32, at_tmp)
        four = place("four", [P, 2, N], F32, at_tmp)
        odd = place("odd", [P, 2, HALF], F32, at_tmp, skip=2 * N)
        rows = place("rows", [P, COLS], F32, at_tmp, skip=2 * N + 2 * HALF)
        hmod = place("hmod", [P, 2, N], F32, at_tmp)

        def small(name, shape):
            words = int(np.prod(shape[1:]))
            return place(name, shape, F32, region(words))

        ident = small("ident", [P, P])
        ones = small("ones", [P, P])
        vecs = small("vecs", [P, P])
        vec_t = small("vec_t", [P, P])
        c_rows = small("c_rows", [DT, P])
        c_exp = small("c_exp", [P, DT])
        c_den = small("c_den", [P, DT])
        c_t = small("c_t", [P, DT])
        silu = small("silu", [P, DT])
        at_silu32 = region(DT * 32)
        silu32 = place("silu32", [P, DT, 32], F32, at_silu32)
        block_junk = place("block_junk", [P, COLS], F32, at_silu32)
        shift32 = place("shift32", [P, DT, 32], F32, at_silu32)
        silu_late = small("silu_late", [P, LATE, 32])
        nyquist = small("nyquist", [P, DT])
        two_tokens = small("two_tokens", [P, 2, DT])
        ssq_part = small("ssq_part", [P, TT, DB])
        mods = small("mods", [P, 6, DT])
        ssq = small("ssq", [P, 3, TT])
        rms = small("rms", [P, 3, TT])
        mean = small("mean", [P, 3, TT])
        inv = small("inv", [P, 3, TT])

        banks = ctx.enter_context(nc.psum_tensor("banks", [P, 8, COLS], F32))

        def sem(name):
            return ctx.enter_context(nc.semaphore(name))

        const_in = sem("const_in")
        acc_zero, brow_in = sem("acc_zero"), sem("brow_in")
        x_in = [sem(f"x_in{t}") for t in range(TT)]
        raw_full = [sem(f"raw_full{s}") for s in range(RAW)]
        ones_set = sem("ones_set")
        turned = sem("turned")
        vec_ready = sem("vec_ready")
        exp_done = sem("exp_done")
        silu_step = sem("silu_step")
        silu_ready = sem("silu_ready")
        sq_done = sem("sq_done")
        mean_done = sem("mean_done")
        rms_done = sem("rms_done")
        inv_done = sem("inv_done")
        xhi_done, xlo_done = sem("xhi_done"), sem("xlo_done")
        table_ready = sem("table_ready")
        spec_sum, spec_done = sem("spec_sum"), sem("spec_done")
        gemv_step = sem("gemv_step")
        col_sum = sem("col_sum")
        gemv_pe = sem("gemv_pe")
        rows_out, rows_turned = sem("rows_out"), sem("rows_turned")
        scale_sum = sem("scale_sum")
        shift_ready, shift_sum = sem("shift_ready"), sem("shift_sum")
        nyquist_ready = sem("nyquist_ready")
        block0_out = sem("block0_out")
        token_step = sem("token_step")
        ssq_sum = sem("ssq_sum")
        gain_done = sem("gain_done")
        table_hi = sem("table_hi")
        mod_step = sem("mod_step")
        modp_hi, modp_lo = sem("modp_hi"), sem("modp_lo")
        chan_sum = sem("chan_sum")
        odd_zero, odd_done = sem("odd_zero"), sem("odd_done")
        four_done, four_hi, four_lo = sem("four_done"), sem("four_hi"), sem("four_lo")
        mirrored = sem("mirrored")
        gate_ready = sem("gate_ready")
        w_hi, w_lo, w_used = sem("w_hi"), sem("w_lo"), sem("w_used")
        y_read = sem("y_read")
        x_updated = sem("x_updated")
        tile_sum = sem("tile_sum")
        tile_gated = sem("tile_gated")
        tile_updated = sem("tile_updated")
        diag_ready = sem("diag_ready")
        h2_turned = sem("h2_turned")
        hmod_done, h2_hi, h2_lo = sem("hmod_done"), sem("h2_hi"), sem("h2_lo")
        h_relu, h_square, h_hi, h_lo = sem("h_relu"), sem("h_square"), sem("h_hi"), sem("h_lo")
        gfin_in = sem("gfin_in")
        y_normed, y_scaled = sem("y_normed"), sem("y_scaled")
        stored = sem("stored")

        HALVES = 2 * HB
        Y1 = DB

        block = ctx.enter_context(nc.Block())

        @block.sync
        def _(sp):
            def unit_source(w, chunk):
                if w[0] == "seq":
                    return seq_table.rearrange("(t p) n -> p t n", p=P)
                if w[0] == "cos":
                    return cos_table.rearrange("(t p) n -> p t n", p=P)
                if w[0] == "sin":
                    return sin_table.rearrange("(t p) n -> p t n", p=P)
                if w[0] == "ada":
                    return ada_v[:, w[2], w[1] * D:(w[1] + 1) * D]
                if w[0] == "mix":
                    return mix_v[:, UK * w[2]:UK * (w[2] + 1), COLS * w[1]:COLS * (w[1] + 1)]
                if w[0] == "up":
                    return up_v[:, UK * w[2]:UK * (w[2] + 1),
                                bass.ds(chunk * CH + COLS * w[1], COLS)]
                return down_v[:, bass.ds(chunk * HT + UK * w[2], UK), COLS * w[1]:COLS * (w[1] + 1)]

            def consumed(w):
                if w in pe_order:
                    return gemv_pe, pe_order.index(w) + 1
                if w[0] == "ada":
                    return gemv_step, ada_order.index(w) + 1
                if w in table_order:
                    return table_ready, table_order.index(w) + 1
                return w_lo, weight_order.index(w) + 1

            def load(w, slot, chunk=0):
                src = unit_source(w, chunk)
                dst = raw[:, slot, :]
                if len(src.shape) == 3:
                    dst = dst[:, 0:src.shape[1] * src.shape[2]].rearrange("p (a n) -> p a n", a=src.shape[1])
                sp.dma_start(dst, src).then_inc(raw_full[slot], 16)

            sp.dma_start(c_rows[:, :], c).then_inc(const_in, 16)
            sp.dma_start(vecs[:, :], vectors).then_inc(const_in, 16)
            for t in range(TT):
                sp.dma_start(xres[:, t, :], x[t * P:(t + 1) * P, :]).then_inc(x_in[t], 16)
            for u, w in enumerate(units):
                if u >= RAW:
                    sp.wait_ge(*consumed(units[u - RAW]))
                load(w, u % RAW)
            with sp.Fori(1, CHUNKS) as chunk:
                for j, w in enumerate(chunk_units):
                    sp.wait_ge(w_lo, chunk * CU + (MU + j - RAW + 1))
                    load(w, slot_of(chunk, j), chunk)
            for t in range(TT):
                sp.wait_ge(y_scaled, t + 1)
                sp.wait_ge(y_normed, t + 1)
                sp.dma_start(out[t * P:(t + 1) * P, :], xres[:, t, :]).then_inc(stored, 16)
            sp.wait_ge(stored, 16 * TT)

        @block.gpsimd
        def _(pool):
            for i in range(2):
                if i == 1:
                    pool.wait_ge(col_sum, 3)
                nc.gpsimd.memset(acc_a[:, :], 0.0).then_inc(acc_zero, 1)
                pool.wait_ge(acc_zero, i + 1)
                pool.dma_start(acc_a[0:1, :], bias_rows[i:i + 1, :]).then_inc(brow_in, 16)
            pool.wait_ge(col_sum, 4)
            pool.dma_start(gfin[:, :], g_final.to_broadcast([P, D])).then_inc(gfin_in, 16)
            pool.wait_ge(gfin_in, 16)
            for d in range(DB - 1):
                cols = slice(COLS * d, COLS * (d + 1))
                pool.wait_ge(x_updated, Y1 + DB * (CHUNKS - 1) + d + 1)
                nc.gpsimd.tensor_tensor(gained[:, :, cols], xres[:, :, cols],
                                        gfin[:, cols].unsqueeze(1).to_broadcast([P, TT, COLS]),
                                        ALU.mult).then_inc(gain_done, 1)
            cols = slice(COLS * (DB - 1), D)
            for t in range(TT):
                if t < TT - 1:
                    pool.wait_ge(tile_updated, TT + t)
                else:
                    pool.wait_ge(x_updated, Y1 + DB * CHUNKS)
                nc.gpsimd.tensor_tensor(gained[:, t, cols], xres[:, t, cols], gfin[:, cols], ALU.mult)\
                    .then_inc(gain_done, 1)

        @block.scalar
        def _(act):
            act.dma_start(ident[:, :], identity).then_inc(const_in, 16)
            act.wait_ge(vec_ready, 1)
            nc.scalar.activation(c_exp[:, :], c_t[:, :], ACT.Exp, scale=-1.0).then_inc(exp_done, 1)

            def root(stage):
                act.wait_ge(mean_done, stage + 1)
                nc.scalar.activation(rms[:, stage, :], mean[:, stage, :], ACT.Sqrt).then_inc(rms_done, 1)

            for t in range(TT):
                act.wait_ge(x_in[t], 16)
                if t >= 1:
                    act.wait_ge(sq_done, t)
                nc.scalar.activation(junk[:, :], xres[:, t, :], ACT.Square,
                                     accum_out=ssq[:, 0, t:t + 1]).then_inc(sq_done, 1)
            root(0)
            act.wait_ge(inv_done, 1)

            def table_high(dst, w):
                u = position[w]
                act.wait_ge(raw_full[u % RAW], filled[u])
                words = dst.shape[1] * dst.shape[2]
                nc.scalar.activation(dst, raw[:, u % RAW, 0:words].rearrange("p (a n) -> p a n", a=dst.shape[1]),
                                     ACT.Copy).then_inc(table_hi, 1)

            def evacuate_spec(d):
                act.wait_ge(spec_sum, d + 1)
                nc.scalar.activation(spec[:, d, :], banks[:, d % 4, :], ACT.Copy).then_inc(spec_done, 1)
                if d == LAST_SCALE:
                    rows_of(0)

            def rows_of(i):
                if i == 0:
                    act.wait_ge(scale_sum, 1)
                elif i == 1:
                    act.wait_ge(gemv_pe, len(pe_order) - LATE)
                elif i == 2:
                    act.wait_ge(shift_sum, 1)
                else:
                    act.wait_ge(col_sum, i - 1)
                if i >= 1:
                    act.wait_ge(rows_turned, i)
                width = FT * P if i == 2 else COLS
                nc.scalar.activation((rows if i < 3 else rows_late)[:, 0:width],
                                     banks[:, (4, 5, 5, 3, 1)[i], 0:width], ACT.Copy)\
                    .then_inc(rows_out, 1)

            def spec_high(g):
                act.wait_ge(mod_step, 3)
                if g >= 2:
                    act.wait_ge(chan_sum, 2 * (g - 1))
                for d in range(GT * g, GT * (g + 1)):
                    nc.scalar.activation(modp[:, (g + 1) % 2, 0, d % GT, :], spec[:, d, :], ACT.Copy,
                                         scale=mods[:, SCALE1, d:d + 1]).then_inc(modp_hi, 1)

            for q in range(GROUPS):
                if q >= 2:
                    act.wait_ge(spec_sum, GT * (q - 1))
                for t in range(TT):
                    nc.scalar.activation(xsp[:, q % 2, 0, t, :], xres[:, t, q * GD:(q + 1) * GD], ACT.Copy,
                                         scale=inv[:, 0, t:t + 1]).then_inc(xhi_done, 1)
                if q == 0:
                    table_high(seqt[:, 0, :, :], ("seq",))
                if q >= 1:
                    for d in range(GT * (q - 1), GT * q):
                        evacuate_spec(d)
            for d in range(GT * (GROUPS - 1), DT):
                evacuate_spec(d)
                if d == DT - 3:
                    table_high(cost[:, 0, :, :], ("cos",))
                if d == DT - 2:
                    spec_high(0)
                    table_high(sint[:, 0, :, :], ("sin",))
            spec_high(1)

            def weight_high(slot, full, ws, used):
                act.wait_ge(raw_full[slot], full)
                if used is not None:
                    act.wait_ge(w_used, used)
                nc.scalar.activation(wsp[:, ws, 0, :, :], raw[:, slot, :].rearrange("p (a n) -> p a n", a=UK),
                                     ACT.Copy).then_inc(w_hi, 1)

            def mix_high(n):
                u = position[("mix",) + mix_units[n]]
                weight_high(u % RAW, filled[u], (n + 1) % WS, n - WS + 1 if n >= WS else None)

            for g in range(GROUPS):
                for h in range(2):
                    if g == GROUPS - 1 and h == 1:
                        act.wait_ge(spec_sum, DT)
                        mix_high(0)
                    s = 2 * g + h
                    act.wait_ge(chan_sum, s + 1)
                    if s == 0:
                        act.wait_ge(odd_zero, 1)
                    if s >= 2:
                        act.wait_ge(four_done, FT * (g - 1) + (1 if h == 0 else FT))
                    nc.scalar.activation(odd[:, h, 1:HALF], banks[:, 2 * h + 1, 1:HALF], ACT.Copy)\
                        .then_inc(odd_done, 1)
                    for r in range(0, 1) if h == 0 else range(1, FT):
                        i = FT * g + r
                        act.wait_ge(four_done, i + 1)
                        nc.scalar.activation(fo[:, GT * g + (0, 1, 3)[r], 0, :], four[:, i % 2, :], ACT.Copy)\
                            .then_inc(four_hi, 1)
                act.wait_ge(four_lo, FT * g + 1)
                first, mirror = fo[:, GT * g, :, :], fo[:, GT * g + 2, :, :]
                nc.scalar.activation(mirror[:, :, 1:N], first[:, :, N - 1:0:-1].bitcast(F32), ACT.Copy)\
                    .then_inc(mirrored, 1)
                nc.scalar.activation(mirror[:, :, 0:1], first[:, :, 0:1].bitcast(F32), ACT.Copy)\
                    .then_inc(mirrored, 1)
                if g + 2 < GROUPS:
                    spec_high(g + 2)

            def block_squares(stage, d, y, tiles=range(TT)):
                if d < DB - 1:
                    act.wait_ge(x_updated, y)
                for t in tiles:
                    if d == DB - 1 and t < TT - 1:
                        act.wait_ge(tile_updated, (TT - 1) * (stage - 1) + t + 1)
                    elif d == DB - 1:
                        act.wait_ge(x_updated, y)
                    if stage_squares[0] > TT:
                        act.wait_ge(sq_done, stage_squares[0])
                    nc.scalar.activation(block_junk[:, :], xres[:, t, COLS * d:COLS * (d + 1)], ACT.Square,
                                         accum_out=ssq_part[:, t, d:d + 1]).then_inc(sq_done, 1)
                    stage_squares[0] += 1

            stage_squares = [TT]

            rows_of(1)
            rows_of(2)
            for n in range(1, MU):
                mix_high(n)
                if n == GATE1_AT - 1:
                    act.wait_ge(w_used, DT // UK)
                    nc.scalar.activation(gated[:, :, :], banks[:, 0:4, :], ACT.Copy).then_inc(block0_out, 1)
                if n == GATE1_AT + 1:
                    act.wait_ge(col_sum, 1)
                    nc.scalar.activation(gate[:, :].rearrange("p (a n) -> p a n", a=DB),
                                         banks[:, 0:4, :], ACT.Copy).then_inc(gate_ready, 1)
                for d in range(DB - 1):
                    if n == UPDATED[d] + 1:
                        block_squares(1, d, d + 1)

            def chunk_high(chunk, j):
                weight_high(slot_of(chunk, j), full_at(chunk, j), (j + 1) % WS, MU + CU * chunk + j - WS + 1)

            chunk_high(0, 0)
            block_squares(1, DB - 1, DB, (0,))
            rows_of(3)
            block_squares(1, DB - 1, DB, range(1, TT))
            root(1)
            rows_of(4)
            act.wait_ge(mod_step, MODS_READY)
            for k in range(DT):
                if k % UK == UK - 1 and k < DT - 1:
                    chunk_high(0, k // UK + 1)
                act.wait_ge(h2_turned, k + 1)
                if k >= 2:
                    act.wait_ge(h2_lo, k - 1)
                nc.scalar.activation(hmod[:, k % 2, :], banks[:, 4 + k % 4, :], ACT.Identity,
                                     scale=mods[:, SCALE2, k:k + 1],
                                     bias=mods[:, SHIFT2, k:k + 1]).then_inc(hmod_done, 1)
                act.wait_ge(hmod_done, k + 1)
                nc.scalar.activation(acts[:, k, 0, :], hmod[:, k % 2, :], ACT.Copy).then_inc(h2_hi, 1)

            def hidden_relu(chunk, g, half):
                h = HALVES * chunk + 2 * g + half
                act.wait_ge(w_used, CU * chunk + (MU + UP_END[g]))
                if half == 0 and g == 0:
                    act.wait_ge(x_updated, Y1 + DB * chunk)
                if half == 0:
                    act.wait_ge(h2_lo, DT)
                if not isinstance(h, int) or h >= 1:
                    act.wait_ge(h_square, h)
                b = 4 * (g % 2) + 2 * half
                nc.scalar.activation(relu[:, :, :], banks[:, b:b + 2, :], ACT.Relu).then_inc(h_relu, 1)

            def hidden_high(chunk, g, half):
                h = HALVES * chunk + 2 * g + half
                act.wait_ge(h_square, h + 1)
                t = 4 * g + 2 * half
                nc.scalar.activation(hid[:, t:t + 2, 0, :], square[:, :, :], ACT.Copy).then_inc(h_hi, 1)

            def chunk_body(chunk):
                for j in range(CU):
                    if not (isinstance(chunk, int) and chunk == 0 and j < DT // UK):
                        if j == DT // UK + 1 or j == 2 * (DT // UK) + 1:
                            if j == 2 * (DT // UK) + 1 and isinstance(chunk, int) and chunk == 0:
                                act.wait_ge(col_sum, 4)
                                nc.scalar.activation(gate[:, :].rearrange("p (a n) -> p a n", a=DB),
                                                     banks[:, 0:4, :], ACT.Copy).then_inc(gate_ready, 1)
                            hidden_relu(chunk, j // (DT // UK) - 1, 0)
                        chunk_high(chunk, j)
                        if j == DT // UK + 1 or j == 2 * (DT // UK) + 1:
                            g = j // (DT // UK) - 1
                            hidden_relu(chunk, g, 1)
                            hidden_high(chunk, g, 0)
                            hidden_high(chunk, g, 1)

            chunk_body(0)
            with act.Fori(1, CHUNKS) as chunk:
                chunk_body(chunk)
            for d in range(DB - 1):
                block_squares(2, d, Y1 + DB * (CHUNKS - 1) + d + 1)

            def scale_tile(t):
                act.wait_ge(inv_done, 3 + t)
                act.wait_ge(gain_done, DB + t)
                nc.scalar.activation(xres[:, t, 0:D // 2], gained[:, t, 0:D // 2], ACT.Copy,
                                     scale=inv[:, 2, t:t + 1]).then_inc(y_scaled, 1)

            for t in range(TT):
                block_squares(2, DB - 1, Y1 + DB * CHUNKS, [t])
                act.wait_ge(mean_done, 3 + t)
                nc.scalar.activation(rms[:, 2, t:t + 1], mean[:, 2, t:t + 1], ACT.Sqrt).then_inc(rms_done, 1)
                scale_tile(t)

        @block.vector
        def _(dve):
            nc.vector.memset(ones[:, :], 1.0).then_inc(ones_set, 1)
            dve.wait_ge(turned, 1)
            nc.vector.tensor_copy(c_t[:, :], banks[:, 1, 0:DT]).then_inc(vec_ready, 1)
            nc.vector.tensor_copy(vec_t[:, :], banks[:, 0, 0:P]).then_inc(vec_ready, 1)
            dve.wait_ge(exp_done, 1)
            nc.vector.tensor_scalar(c_den[:, :], c_exp[:, :], 1.0, None, ALU.add).then_inc(silu_step, 1)
            dve.wait_ge(silu_step, 1)
            nc.vector.reciprocal(c_exp[:, :], c_den[:, :]).then_inc(silu_step, 1)
            dve.wait_ge(silu_step, 2)
            nc.vector.tensor_tensor(silu[:, :], c_t[:, :], c_exp[:, :], ALU.mult).then_inc(silu_step, 1)
            dve.wait_ge(silu_step, 3)
            nc.vector.tensor_copy(silu_late[:, :, :], silu[:, DT - LATE:].unsqueeze(2).to_broadcast([P, LATE, 32]))
            nc.vector.tensor_copy(silu32[:, :, :], silu[:, :].unsqueeze(2).to_broadcast([P, DT, 32]))\
                .then_inc(silu_ready, 1)

            def inverse(stage):
                dve.wait_ge(sq_done, TT + DB * TT * stage)
                if stage >= 1:
                    nc.vector.tensor_reduce(ssq[:, stage, :], ssq_part[:, :, :], mybir.AxisListType.X, ALU.add)\
                        .then_inc(ssq_sum, 1)
                    dve.wait_ge(ssq_sum, stage)
                nc.vector.tensor_scalar(mean[:, stage, :], ssq[:, stage, :], 1.0 / D, EPS,
                                        ALU.mult, ALU.add).then_inc(mean_done, 1)
                dve.wait_ge(rms_done, stage + 1)
                nc.vector.reciprocal(inv[:, stage, :], rms[:, stage, :]).then_inc(inv_done, 1)
                dve.wait_ge(inv_done, stage + 1)

            steps = [0]

            def gemv(j, k):
                u = position[("ada", j, k)]
                s = u % RAW
                acc = {SCALE1: acc_s, SHIFT2: acc_b}.get(j, acc_a)
                if k == 0:
                    if j == SHIFT2:
                        dve.wait_ge(chan_sum, 2 * GROUPS)
                    elif j in (SCALE2, GATE2):
                        dve.wait_ge(col_sum, {SCALE2: 1, GATE2: 3}[j])
                    if j in (GATE1, GATE2):
                        dve.wait_ge(brow_in, 16 * (1 + (j == GATE2)))
                dve.wait_ge(raw_full[s], filled[u])
                if k == 0 and j not in (GATE1, GATE2):
                    ins = nc.vector.tensor_scalar(acc[:, :], raw[:, s, :], silu[:, 0:1], None, ALU.mult)
                else:
                    if steps[0] >= 1:
                        dve.wait_ge(gemv_step, steps[0])
                    ins = nc.vector.scalar_tensor_tensor(acc[:, :], raw[:, s, :], silu[:, k:k + 1], acc[:, :],
                                                         ALU.mult, ALU.add)
                ins.then_inc(gemv_step, 1)
                steps[0] += 1

            def table_low(dst, hi, w, n):
                u = position[w]
                dve.wait_ge(table_hi, n)
                words = dst.shape[1] * dst.shape[2]
                nc.vector.tensor_tensor(dst, raw[:, u % RAW, 0:words].rearrange("p (a n) -> p a n", a=dst.shape[1]),
                                        hi.bitcast(F32), ALU.subtract).then_inc(table_ready, 1)

            def x_low(q):
                for t in range(TT):
                    dve.wait_ge(xhi_done, TT * q + t + 1)
                    nc.vector.scalar_tensor_tensor(
                        xsp[:, q % 2, 1, t, :], xres[:, t, q * GD:(q + 1) * GD], inv[:, 0, t:t + 1],
                        xsp[:, q % 2, 0, t, :].bitcast(F32), ALU.mult, ALU.subtract).then_inc(xlo_done, 1)

            inverse(0)
            x_low(0)
            table_low(seqt[:, 1, :, :], seqt[:, 0, :, :], ("seq",), 1)
            scale_left = [k for k in range(DT) if k % SHARE != SHARE - 1]
            for q, count in zip(range(1, GROUPS + 1), (1, 4, 3, len(scale_left))):
                for _ in range(min(count, len(scale_left))):
                    gemv(SCALE1, scale_left.pop(0))
                if q < GROUPS:
                    x_low(q)

            def times_gain(j, gain):
                nc.vector.scalar_tensor_tensor(mods[:, j, :], mods[:, j, :], 1.0, gain, ALU.add,
                                               ALU.mult).then_inc(mod_step, 1)

            def turned_rows(j, bank):
                dve.wait_ge(vec_ready, 2)
                sums = banks[:, bank, :].rearrange("p (b a r) -> p a b r", b=4, a=4)[:, :, :, 0]
                nc.vector.tensor_tensor(mods[:, j, :].rearrange("p (a b) -> p a b", a=4), sums,
                                        vec_t[:, j * DT:(j + 1) * DT].rearrange("p (a b) -> p a b", a=4),
                                        ALU.add).then_inc(mod_step, 1)

            dve.wait_ge(rows_turned, 1)
            turned_rows(SCALE1, 6)
            dve.wait_ge(mod_step, 1)
            times_gain(SCALE1, vec_t[:, 6 * DT:7 * DT])
            dve.wait_ge(mod_step, 2)
            nc.vector.tensor_scalar(mods[:, SCALE1, :], mods[:, SCALE1, :], NORM, None, ALU.mult)\
                .then_inc(mod_step, 1)
            dve.wait_ge(mod_step, 3)
            nc.vector.memset(odd[:, :, 0:1], 0.0).then_inc(odd_zero, 1)
            nc.vector.memset(four[:, :, HALF:HALF + 1], 0.0)

            def spec_low(g):
                for d in range(GT * g, GT * (g + 1)):
                    dve.wait_ge(modp_hi, d + 1)
                    nc.vector.scalar_tensor_tensor(
                        modp[:, (g + 1) % 2, 1, d % GT, :], spec[:, d, :], mods[:, SCALE1, d:d + 1],
                        modp[:, (g + 1) % 2, 0, d % GT, :].bitcast(F32), ALU.mult, ALU.subtract).then_inc(modp_lo, 1)

            def four_tile(i):
                g, kind = i // FT, i % FT
                tile = GT * g + (0, 1, 3)[kind]
                h = 0 if kind == 0 else 1
                dve.wait_ge(odd_done, 2 * g + h + 1)
                even = banks[:, (0, 2, 6)[kind], :]
                if i >= 2:
                    dve.wait_ge(four_lo, i - 1)
                    dve.wait_ge(four_hi, i - 1)
                near, far = (ALU.subtract, ALU.add) if kind < 2 else (ALU.add, ALU.subtract)
                nc.vector.tensor_tensor(four[:, i % 2, 0:HALF], even[:, 0:HALF], odd[:, h, :], near)
                nc.vector.tensor_tensor(four[:, i % 2, N - 1:HALF:-1], even[:, 1:HALF], odd[:, h, 1:HALF], far)\
                    .then_inc(four_done, 1)
                dve.wait_ge(four_hi, i + 1)
                nc.vector.tensor_tensor(fo[:, tile, 1, :], four[:, i % 2, :], fo[:, tile, 0, :].bitcast(F32),
                                        ALU.subtract).then_inc(four_lo, 1)

            table_low(cost[:, 1, :, :], cost[:, 0, :, :], ("cos",), 2)
            spec_low(0)
            table_low(sint[:, 1, :, :], sint[:, 0, :, :], ("sin",), 3)
            spec_low(1)
            dve.wait_ge(spec_done, DT)
            nc.vector.tensor_tensor(nyquist[:, :], spec[:, :, HALF], mods[:, SCALE1, :], ALU.mult)\
                .then_inc(nyquist_ready, 1)
            def weight_low(slot, ws, n):
                dve.wait_ge(w_hi, n + 1)
                nc.vector.tensor_tensor(wsp[:, ws, 1, :, :],
                                        raw[:, slot, :].rearrange("p (a n) -> p a n", a=UK),
                                        wsp[:, ws, 0, :, :].bitcast(F32), ALU.subtract).then_inc(w_lo, 1)

            def shift_vector():
                dve.wait_ge(rows_turned, 2)
                turned_rows(SHIFT1, 7)
                dve.wait_ge(mod_step, 4)
                nc.vector.tensor_scalar(mods[:, SHIFT1, :], mods[:, SHIFT1, :], N * NORM, None, ALU.mult)\
                    .then_inc(mod_step, 1)
                dve.wait_ge(mod_step, MODS1)
                dve.wait_ge(nyquist_ready, 1)
                for i, vector in enumerate((mods[:, SHIFT1, :], nyquist[:, :])):
                    nc.vector.tensor_copy(shift32[:, :, 16 * i:16 * (i + 1)],
                                          vector.unsqueeze(2).to_broadcast([P, DT, 16])).then_inc(shift_ready, 1)

            def mix_low(n):
                weight_low(position[("mix",) + mix_units[n]] % RAW, (n + 1) % WS, n)

            for i in range(GROUPS * FT):
                if i == GROUPS * FT - 2:
                    mix_low(0)
                four_tile(i)
                if i % FT == FT - 1 and i // FT + 2 < GROUPS:
                    spec_low(i // FT + 2)
            shift_vector()
            def shift_token():
                dve.wait_ge(mirrored, 2 * GROUPS)
                nc.vector.tensor_tensor(two_tokens[:, 0, :], fo[:, :, 0, 0].bitcast(F32), fo[:, :, 1, 0].bitcast(F32),
                                        ALU.add).then_inc(token_step, 1)
                dve.wait_ge(rows_turned, 3)
                dve.wait_ge(token_step, 1)
                sums = banks[:, 7, 0:FT * P].rearrange("p (b g r) -> p g b r", b=FT, g=GROUPS)
                tiles = two_tokens[:, :, :].rearrange("p t (g i) -> p t g i", g=GROUPS)
                for i, kinds in ((0, slice(0, 2)), (2, slice(0, 3, 2))):
                    nc.vector.tensor_tensor(tiles[:, 0, :, i:i + 2], tiles[:, 0, :, i:i + 2], sums[:, :, kinds, 0],
                                            ALU.add).then_inc(token_step, 1)
                    nc.vector.tensor_copy(tiles[:, 1, :, i:i + 2], sums[:, :, kinds, 16]).then_inc(token_step, 1)
                dve.wait_ge(token_step, 5)
                both = two_tokens[:, :, :].rearrange("p t d -> p d t")
                nc.vector.tensor_copy(fo[:, :, 0, 0:N:HALF], both).then_inc(token_step, 1)
                dve.wait_ge(token_step, 6)
                nc.vector.tensor_tensor(fo[:, :, 1, 0:N:HALF], both, fo[:, :, 0, 0:N:HALF].bitcast(F32),
                                        ALU.subtract).then_inc(token_step, 1)

            def update_x(y, b, d, gates, done, source=None):
                dve.wait_ge(w_used, done)
                dve.wait_ge(gate_ready, gates)
                if not isinstance(y, int) or y >= 1:
                    dve.wait_ge(x_updated, y)
                cols = slice(COLS * d, COLS * (d + 1))
                nc.vector.tensor_tensor(gated[:, :, :], banks[:, b:b + 4, :] if source is None else source,
                                        gate[:, cols].unsqueeze(1).to_broadcast([P, TT, COLS]),
                                        ALU.mult).then_inc(y_read, 1)
                dve.wait_ge(y_read, y + 1)
                nc.vector.tensor_tensor(xres[:, :, cols], xres[:, :, cols], gated[:, :, :],
                                        ALU.add).then_inc(x_updated, 1)

            def update_tiles(i, y, gates, done, after=None):
                d = DB - 1
                before = (TT - 1) * CHUNKS * i
                cols = slice(COLS * d, COLS * (d + 1))
                dve.wait_ge(gate_ready, gates)
                dve.wait_ge(x_updated, y)
                for t in range(TT):
                    last = t == TT - 1
                    if last:
                        dve.wait_ge(w_used, done)
                    else:
                        dve.wait_ge(tile_sum, before + t + 1)
                    nc.vector.tensor_tensor(gated[:, t, :], banks[:, 4 + t, :], gate[:, cols], ALU.mult)\
                        .then_inc(y_read if last else tile_gated, 1)
                    if last:
                        dve.wait_ge(y_read, y + 1)
                    else:
                        dve.wait_ge(tile_gated, (TT - 1) * i + t + 1)
                    nc.vector.tensor_tensor(xres[:, t, cols], xres[:, t, cols], gated[:, t, :], ALU.add)\
                        .then_inc(x_updated if last else tile_updated, 1)
                    if after is not None:
                        after(t)

            def run_gemvs(n, first=0, last=DT):
                for _, j, k in runs[n][first:last]:
                    gemv(j, k)

            for n in range(MU):
                if n >= 1:
                    mix_low(n)
                if n == 0:
                    run_gemvs(0, 0, 2)
                    shift_token()
                    run_gemvs(0, 2)
                elif n < MU - 1:
                    run_gemvs(n)
                if n in UPDATED:
                    y = UPDATED.index(n)
                    if y == 0:
                        dve.wait_ge(block0_out, 1)
                    update_x(y, 4 * (y % 2), y, 1, (y + 1) * (DT // UK), gated[:, :, :] if y == 0 else None)
            weight_low(slot_of(0, 0), 1, MU)
            update_tiles(0, DB - 1, 1, MU)
            inverse(1)
            nc.vector.tensor_tensor(diag[:, :, :], ident[:, :].unsqueeze(1).to_broadcast([P, TT, P]),
                                    inv[:, 1, :].unsqueeze(2).to_broadcast([P, TT, P]), ALU.mult)\
                .then_inc(diag_ready, 1)
            dve.wait_ge(rows_turned, 4)
            turned_rows(SHIFT2, 0)
            dve.wait_ge(rows_turned, 5)
            turned_rows(SCALE2, 2)
            dve.wait_ge(mod_step, MODS_READY - 1)
            times_gain(SCALE2, vec_t[:, 7 * DT:8 * DT])

            def gate2(j):
                for k in range(per_up * j, per_up * (j + 1)):
                    gemv(GATE2, k)

            for k in range(DT):
                if k % UK == UK - 1 and k < DT - 1:
                    j = k // UK + 1
                    weight_low(slot_of(0, j), (j + 1) % WS, MU + j)
                    gate2(j - 1)
                dve.wait_ge(h2_hi, k + 1)
                nc.vector.tensor_tensor(acts[:, k, 1, :], hmod[:, k % 2, :], acts[:, k, 0, :].bitcast(F32),
                                        ALU.subtract).then_inc(h2_lo, 1)

            def hidden_square(chunk, g, half):
                h = HALVES * chunk + 2 * g + half
                dve.wait_ge(h_relu, h + 1)
                if not isinstance(h, int) or h >= 1:
                    dve.wait_ge(h_lo, h)
                nc.vector.tensor_tensor(square[:, :, :], relu[:, :, :], relu[:, :, :], ALU.mult)\
                    .then_inc(h_square, 1)

            def hidden_low(chunk, g, half):
                h = HALVES * chunk + 2 * g + half
                dve.wait_ge(h_hi, h + 1)
                t = 4 * g + 2 * half
                nc.vector.tensor_tensor(hid[:, t:t + 2, 1, :], square[:, :, :], hid[:, t:t + 2, 0, :].bitcast(F32),
                                        ALU.subtract).then_inc(h_lo, 1)

            def chunk_body(chunk):
                first = isinstance(chunk, int) and chunk == 0
                for j in range(CU):
                    hidden = j == DT // UK + 1 or j == 2 * (DT // UK) + 1
                    g = j // (DT // UK) - 1
                    if hidden:
                        hidden_square(chunk, g, 0)
                    if not (first and j < DT // UK):
                        weight_low(slot_of(chunk, j), (j + 1) % WS, MU + CU * chunk + j)
                    if hidden:
                        hidden_low(chunk, g, 0)
                        hidden_square(chunk, g, 1)
                        hidden_low(chunk, g, 1)
                    if first and DT // UK - 1 <= j < len(up_units):
                        gate2(j)
                    if j == 1 and not first:
                        update_x(DB * chunk + (Y1 - 1), 4, DB - 1, 2, CU * chunk + MU)
                    for d in range(DB - 1):
                        if j == DOWN_END[d] + 1:
                            update_x(DB * chunk + (Y1 + d), 4 * (d % 2), d, 2, CU * chunk + (MU + DOWN_END[d]))

            chunk_body(0)
            with dve.Fori(1, CHUNKS) as chunk:
                chunk_body(chunk)

            def scale_half(t):
                dve.wait_ge(inv_done, 3 + t)
                dve.wait_ge(gain_done, DB + t)
                nc.vector.tensor_scalar(xres[:, t, D // 2:], gained[:, t, D // 2:], inv[:, 2, t:t + 1], None,
                                        ALU.mult).then_inc(y_normed, 1)

            def invert_tile(t):
                if t >= 1:
                    scale_half(t - 1)
                dve.wait_ge(sq_done, TT + DB * TT + (DB - 1) * TT + t + 1)
                nc.vector.tensor_reduce(ssq[:, 2, t:t + 1], ssq_part[:, t, :], mybir.AxisListType.X, ALU.add)\
                    .then_inc(ssq_sum, 1)
                dve.wait_ge(ssq_sum, 2 + t)
                nc.vector.tensor_scalar(mean[:, 2, t:t + 1], ssq[:, 2, t:t + 1], 1.0 / D, EPS,
                                        ALU.mult, ALU.add).then_inc(mean_done, 1)
                dve.wait_ge(rms_done, 3 + t)
                nc.vector.reciprocal(inv[:, 2, t:t + 1], rms[:, 2, t:t + 1]).then_inc(inv_done, 1)

            update_tiles(1, Y1 + DB * CHUNKS - 1, 2, MU + CU * CHUNKS, invert_tile)
            scale_half(TT - 1)

        @block.tensor
        def _(pe):
            def product(bank, w_hi_ap, w_lo_ap, m_hi, m_lo, first, last):
                nc.tensor.matmul(bank, w_hi_ap, m_hi, start=first, stop=False)
                nc.tensor.matmul(bank, w_hi_ap, m_lo, start=False, stop=False)
                return nc.tensor.matmul(bank, w_lo_ap, m_hi, start=False, stop=last)

            pe.wait_ge(const_in, 48)
            nc.tensor.transpose(banks[:, 0, 0:P], vecs[:, :], ident[:, :])
            nc.tensor.transpose(banks[:, 1, 0:DT], c_rows[:, :], ident[0:DT, 0:DT]).then_inc(turned, 1)
            pe.wait_ge(vec_ready, 2)

            def gemv_rows(j, k):
                u = position[("ada", j, k)]
                bank, first = {SCALE1: (4, SHARE - 1), SHIFT1: (5, 0), SCALE2: (1, DT - LATE)}[j]
                silus = silu_late[:, k - DT + LATE, :] if j == SCALE2 else silu32[:, k, :]
                pe.wait_ge(raw_full[u % RAW], filled[u])
                for a in range(4):
                    mm = nc.tensor.matmul(banks[32 * a:32 * (a + 1), bank, :], silus,
                                          raw[:, u % RAW, COLS * a:COLS * (a + 1)], start=(k == first),
                                          stop=(j == SHIFT1 and k == DT - 1))
                mm.then_inc(gemv_pe, 1)

            def add_share(bank, acc, whole=False):
                for a in range(4):
                    mm = nc.tensor.matmul(banks[32 * a:32 * (a + 1), bank, :], ones[:, 0:32],
                                          acc[:, COLS * a:COLS * (a + 1)], start=whole, stop=True)
                return mm

            def turn_rows(i, bank, blocks=4):
                pe.wait_ge(rows_out, i + 1)
                source = rows if i < 3 else rows_late
                for b in range(blocks):
                    mm = nc.tensor.transpose(banks[:, bank, P * b:P * (b + 1)], source[:, P * b:P * (b + 1)],
                                             ident[:, :])
                mm.then_inc(rows_turned, 1)

            pe.wait_ge(silu_ready, 1)
            pe.wait_ge(table_ready, 1)
            for d in range(DT):
                q = d // GT
                pe.wait_ge(xlo_done, TT * (q + 1))
                if d >= 4:
                    pe.wait_ge(spec_done, d - 3)
                cols = slice(P * (d % GT), P * (d % GT + 1))
                for t in range(TT):
                    mm = product(banks[:, d % 4, :], xsp[:, q % 2, 0, t, cols], xsp[:, q % 2, 1, t, cols],
                                 seqt[:, 0, t, :], seqt[:, 1, t, :], t == 0, t == TT - 1)
                mm.then_inc(spec_sum, 1)
                if d % SHARE == 0:
                    gemv_rows(SCALE1, d + SHARE - 1)
                if d == LAST_SCALE:
                    pe.wait_ge(ones_set, 1)
                    pe.wait_ge(gemv_step, SCALE1_STEPS)
                    add_share(4, acc_s).then_inc(scale_sum, 1)
                if d == LAST_SCALE + 1:
                    turn_rows(0, 6)

            def row_sums(acc, bank):
                for d in range(DB):
                    mm = nc.tensor.matmul(banks[:, bank + d, :], ones[:, :], acc[:, COLS * d:COLS * (d + 1)],
                                          start=True, stop=True)
                mm.then_inc(col_sum, 1)

            shift_tiles = list(range(DT))
            for _ in range(2):
                gemv_rows(SHIFT1, shift_tiles.pop(0))
            pe.wait_ge(table_ready, 2)
            pe.wait_ge(spec_done, DT)
            for g in range(GROUPS):
                pe.wait_ge(modp_lo, GT * (g + 1))
                for h in range(2):
                    if g >= 1:
                        pe.wait_ge(four_done, FT * (g - 1) + (1 if h == 0 else FT))
                    if g == 0 and h == 1:
                        pe.wait_ge(mod_step, 1)
                    for kind, bank in ((0, 0),) if h == 0 else ((1, 2), (2, 6)):
                        cols = slice(P * kind, P * (kind + 1))
                        for d in range(GT):
                            product(banks[:, bank, 0:HALF], cost[:, 0, d, cols], cost[:, 1, d, cols],
                                    modp[:, (g + 1) % 2, 0, d, 0:HALF], modp[:, (g + 1) % 2, 1, d, 0:HALF],
                                    d == 0, d == GT - 1)
                    cols = slice(P * h, P * (h + 1))
                    if g == 0 and h == 0:
                        pe.wait_ge(table_ready, 3)
                    for d in range(GT):
                        mm = product(banks[:, 2 * h + 1, 0:HALF], sint[:, 0, d, cols], sint[:, 1, d, cols],
                                     modp[:, (g + 1) % 2, 0, d, HALF:], modp[:, (g + 1) % 2, 1, d, HALF:],
                                     d == 0, d == GT - 1)
                    mm.then_inc(chan_sum, 1)
                    for _ in range((1, 1, 2, 1)[(2 * g + h) % 4]):
                        gemv_rows(SHIFT1, shift_tiles.pop(0))

            def transform_shift():
                pe.wait_ge(shift_ready, 2)
                for d in range(GT):
                    for part in range(2):
                        for g in range(GROUPS):
                            mm = nc.tensor.matmul(banks[32 * g:32 * (g + 1), 5, 0:FT * P],
                                                  shift32[:, GT * g + d, :], cost[:, part, d, :].bitcast(F32),
                                                  start=(d == 0 and part == 0), stop=(d == GT - 1 and part == 1))
                mm.then_inc(shift_sum, 1)

            def token_unit(b, ws, n, left, q, k_tiles, by_tile=False, tiles=range(TT), steps={}):
                pe.wait_ge(w_lo, n + 1)
                for i in range(TT):
                    t = tiles[i]
                    if i in steps:
                        steps[i]()
                    tok = slice(P * t, P * (t + 1))
                    for kk in range(UK):
                        k = UK * q + kk
                        mm = product(banks[:, b + t, :], left[:, k, 0, tok], left[:, k, 1, tok],
                                     wsp[:, ws, 0, kk, :], wsp[:, ws, 1, kk, :], k == 0, k == k_tiles - 1)
                    if by_tile and t < TT - 1:
                        mm.then_inc(tile_sum, 1)
                mm.then_inc(w_used, 1)

            def shift_end():
                for k in shift_tiles[SHIFT_LAST // 2:]:
                    gemv_rows(SHIFT1, k)
                turn_rows(1, 7)

            def patch():
                transform_shift()
                turn_rows(2, 7, FT)
                pe.wait_ge(token_step, 7)

            assert len(shift_tiles) == SHIFT_LAST
            for k in shift_tiles[:SHIFT_LAST // 2]:
                gemv_rows(SHIFT1, k)
            patch_steps = {1: shift_end, 2: patch}
            def late_step(i):
                if i == 1:
                    pe.wait_ge(gemv_step, SCALE1_STEPS + 2 * DT)
                    add_share(3, acc_b, True).then_inc(col_sum, 1)
                elif i == 3:
                    turn_rows(3, 0)
                gemv_rows(SCALE2, DT - LATE + i - 1)

            late_steps = {i: lambda i=i: late_step(i) for i in range(1, TT)}
            for n, (d, q) in enumerate(mix_units):
                if q == 0:
                    if d == 0:
                        pe.wait_ge(four_done, FT * GROUPS)
                        pe.wait_ge(mirrored, 2)
                        pe.wait_ge(four_lo, FT)
                    elif d == 2:
                        pe.wait_ge(gate_ready, 1)
                    elif d == 3:
                        pe.wait_ge(y_read, 2)
                if n == MU - 1:
                    pe.wait_ge(y_read, DB - 1)
                if n == GATE1_AT:
                    pe.wait_ge(block0_out, 1)
                    pe.wait_ge(gemv_step, SCALE1_STEPS + DT)
                    row_sums(acc_a, 0)
                token_unit(4 * (d % 2), (n + 1) % WS, n, fo, q, DT, by_tile=n == MU - 1,
                           tiles=(1, 3, 2, 0) if n == 0 else range(TT), steps={0: patch_steps, MU - 1: late_steps}.get(n, {}))

            def turn_tokens(k):
                if k >= 4:
                    pe.wait_ge(hmod_done, k - 3)
                for t in range(TT):
                    mm = nc.tensor.matmul(banks[:, 4 + k % 4, P * t:P * (t + 1)],
                                          xres[:, t, P * k:P * (k + 1)], diag[:, t, :], start=(t == 0), stop=True,
                                          skip_group_check=True)
                mm.then_inc(h2_turned, 1)

            LEAD = 3
            gemv_rows(SCALE2, DT - 2)
            gemv_rows(SCALE2, DT - 1)
            pe.wait_ge(gemv_step, SCALE1_STEPS + 3 * DT - LATE)
            add_share(1, acc_a).then_inc(col_sum, 1)
            pe.wait_ge(diag_ready, 1)
            turn_tokens(0)
            turn_rows(4, 2)
            for k in range(1, LEAD):
                turn_tokens(k)

            def chunk_body(chunk):
                first = isinstance(chunk, int) and chunk == 0
                for j, (what, a, q) in enumerate(chunk_units):
                    n = MU + CU * chunk + j
                    b = 4 * (a % 2)
                    if what == "up":
                        if q == 0:
                            pe.wait_ge(y_read, Y1 + DB * chunk - 1 + a)
                            if first and a == 0:
                                pe.wait_ge(mod_step, MODS_READY)
                        pe.wait_ge(w_lo, n + 1)
                        for kk in range(UK):
                            k = UK * q + kk
                            if first and a == 0:
                                if k + LEAD < DT:
                                    turn_tokens(k + LEAD)
                                pe.wait_ge(h2_lo, k + 1)
                            for f in range(4):
                                cols = slice(P * f, P * (f + 1))
                                mm = product(banks[:, b + f, :], wsp[:, (j + 1) % WS, 0, kk, cols],
                                             wsp[:, (j + 1) % WS, 1, kk, cols], acts[:, k, 0, :], acts[:, k, 1, :],
                                             k == 0, k == DT - 1)
                        mm.then_inc(w_used, 1)
                        if first and j == len(up_units) - 1:
                            pe.wait_ge(h_relu, 2)
                            pe.wait_ge(gemv_step, SCALE1_STEPS + 4 * DT - LATE)
                            row_sums(acc_a, 0)
                            pe.wait_ge(gate_ready, 2)
                    else:
                        if q == 0:
                            if a < 2:
                                pe.wait_ge(h_relu, HALVES * chunk + 2 * (a + 1))
                            else:
                                pe.wait_ge(y_read, Y1 + DB * chunk + a - 1)
                        pe.wait_ge(h_lo, HALVES * chunk + 2 * (q + 1))
                        token_unit(b, (j + 1) % WS, n, hid, q, HT, by_tile=j == CU - 1)

            chunk_body(0)
            with pe.Fori(1, CHUNKS) as chunk:
                chunk_body(chunk)


INPUTS = ("x", "c", "w_ada", "vectors", "bias_rows", "g_final", "w_mix", "w_ffn_in", "w_ffn_out",
          "seq_table", "cos_table", "sin_table", "identity")


def fourier_tables(n):
    a = np.arange(n)
    angle = 2 * np.pi * (np.outer(a, a) % n) / n
    cos, sin = np.cos(angle), np.sin(angle)
    half = n // 2
    seq = np.concatenate([cos[:, :half + 1], sin[:, 1:half]], axis=1)
    kept = np.concatenate([cos[:, 1:half + 1], cos[:, half // 2 + 1:half], cos[:, :1]], axis=1)
    return [t.astype(np.float32) for t in (seq, kept, sin[:, 1:half + 1])]


def mirrored_rows(w, groups):
    size = w.shape[0] // groups
    half = size // 2
    order = np.r_[1:half + 1, size - 1:half:-1, 0]
    return w.reshape(groups, size, -1)[:, order].reshape(w.shape)


def kernel(**inputs):
    import concourse.bacc as bacc
    from concourse.bass_utils import run_bass_kernel_spmd

    a = {k: np.ascontiguousarray(np.asarray(v)) for k, v in inputs.items()}
    n, d = a["x"].shape[1:]
    b_ada = a["b_ada"][0]
    seq_table, cos_table, sin_table = fourier_tables(n)
    data = {
        "x": a["x"][0], "c": a["c"].reshape(d // 128, 128), "w_ada": a["w_ada"][0],
        "vectors": np.concatenate([b_ada, a["g_norm_mix"][0], a["g_norm_ffn"][0]]).reshape(-1, 128),
        "bias_rows": np.stack([b_ada[2 * d:3 * d], b_ada[5 * d:6 * d]]),
        "g_final": a["g_final"].reshape(1, d), "w_mix": mirrored_rows(a["fno_w_out"][0], 4),
        "w_ffn_in": a["w_ffn_in"][0], "w_ffn_out": a["w_ffn_out"][0],
        "seq_table": seq_table, "cos_table": cos_table, "sin_table": sin_table, "identity": np.eye(128, dtype=np.float32),
    }
    data = {f"in_{k}": np.ascontiguousarray(data[k]) for k in INPUTS}
    nc = bacc.Bacc("TRN2", target_bir_lowering=False, num_devices=1, dynamic_dma_scratch_size=1024)
    aps = [nc.dram_tensor(k, v.shape, mybir.dt.from_np(v.dtype), kind="ExternalInput").ap()
           for k, v in data.items()]
    out = nc.dram_tensor("out", (n, d), mybir.dt.float32, kind="ExternalOutput").ap()
    fourier_ffn_block(nc, *aps, out)
    result = run_bass_kernel_spmd(nc, [data], core_ids=[0])
    return result.results[0]["out"].reshape(1, n, d)
```
